# Optimizing a Trainium2 kernel written in Bass

```python
import math
import jax, jax.numpy as jnp
from jax import lax
import numpy as np
import jax
import jax.numpy as jnp

D_MODEL = 1024
BATCH = 1
SEQ = 1024
DEPTH = 2

GLA_HEADS = 4
GLA_DK = 32
GLA_DV = 64
GLA_RANK = 16
GLA_GATE_TEMP = 16.0
DIFF_HEADS = 4
DIFF_HD = 64
DIFF_DV = 2 * DIFF_HD
HGRN_HEADS = 4
HGRN_DK = 64
HGRN_DV = 64
CHUNK = 16
Q_BLOCK = 128
ROPE_THETA = 10000.0
EPS = 1e-6
F_FLOOR = 1e-30

GLA_W = GLA_HEADS * GLA_DV
DIFF_W = DIFF_HEADS * DIFF_DV
HGRN_W = HGRN_HEADS * HGRN_DV
MIX_W = GLA_W + DIFF_W + HGRN_W

IN_SIZES = (
    GLA_HEADS * GLA_DK, GLA_HEADS * GLA_DK, GLA_W, GLA_W, GLA_RANK, GLA_RANK,
    DIFF_HEADS * 2 * DIFF_HD, DIFF_HEADS * 2 * DIFF_HD, DIFF_W, DIFF_W,
    HGRN_HEADS * HGRN_DK, HGRN_HEADS * HGRN_DK, HGRN_HEADS * HGRN_DK, HGRN_W, HGRN_W,
)
IN_W = sum(IN_SIZES)


def _offsets():
    offs, run = [], 0
    for s in IN_SIZES[:-1]:
        run += s
        offs.append(run)
    return offs

def rms_norm(x, w):
    xf = x.astype(jnp.float32)
    xf = xf * lax.rsqrt(jnp.mean(xf * xf, axis=-1, keepdims=True) + EPS)
    return xf.astype(x.dtype) * w

def split_heads(t, n_heads):
    b, l, _ = t.shape
    return t.reshape(b, l, n_heads, -1).transpose(0, 2, 1, 3)

def merge_heads(t):
    b, h, l, d = t.shape
    return t.transpose(0, 2, 1, 3).reshape(b, l, h * d)

def rope(x, pos):
    d = x.shape[-1]
    inv_freq = ROPE_THETA ** (-jnp.arange(0, d, 2, dtype=jnp.float32) / d)
    ang = pos.astype(jnp.float32)[:, None] * inv_freq[None, :]
    cos, sin = jnp.cos(ang).astype(x.dtype), jnp.sin(ang).astype(x.dtype)
    x1, x2 = x[..., : d // 2], x[..., d // 2:]
    return jnp.concatenate([x1 * cos - x2 * sin, x2 * cos + x1 * sin], axis=-1)

def chunked_gated_scan(q, k, v, log_g):
    b_, h_, l_, dk = q.shape
    dv = v.shape[-1]
    n = l_ // CHUNK
    r = lambda t: t.reshape(b_, h_, n, CHUNK, t.shape[-1])
    q, k, v, lg = r(q), r(k), r(v), r(log_g)
    bcum = jnp.cumsum(lg.astype(jnp.float32), axis=3)
    mask = jnp.tril(jnp.ones((CHUNK, CHUNK), dtype=bool))[:, :, None]
    diff = bcum[:, :, :, :, None, :] - bcum[:, :, :, None, :, :]
    decay = jnp.where(mask, jnp.exp(jnp.where(mask, diff, 0.0)), 0.0)
    attn = jnp.einsum('bhntk,bhnsk,bhntsk->bhnts', q, k, decay.astype(q.dtype))
    o_intra = jnp.einsum('bhnts,bhnsv->bhntv', attn, v)
    b_last = bcum[:, :, :, -1:, :]
    u = jnp.einsum('bhnsk,bhnsv->bhnkv', k * jnp.exp(b_last - bcum).astype(k.dtype), v)
    g_chunk = jnp.exp(b_last[:, :, :, 0, :]).astype(u.dtype)

    def step(state, inp):
        g_n, u_n = inp
        return g_n[..., None] * state + u_n, state

    s0 = jnp.zeros((b_, h_, dk, dv), u.dtype)
    _, s_prev = lax.scan(step, s0, (jnp.moveaxis(g_chunk, 2, 0), jnp.moveaxis(u, 2, 0)))
    s_prev = jnp.moveaxis(s_prev, 0, 2)
    o_inter = jnp.einsum('bhntk,bhnkv->bhntv', q * jnp.exp(bcum).astype(q.dtype), s_prev)
    return (o_intra + o_inter).reshape(b_, h_, l_, dv).astype(v.dtype)

def bidir_scan(q, k_f, k_b, v, lg_f, lg_b):
    flip = lambda t: jnp.flip(t, axis=2)
    o_f = chunked_gated_scan(q, k_f, v, lg_f)
    o_b = flip(chunked_gated_scan(flip(q), flip(k_b), flip(v), flip(lg_b)))
    return o_f + o_b

def gla_branch(q, k, v, g, a_f, a_b, wa2_f, ba_f, wa2_b, ba_b, norm_w):
    q = split_heads(q, GLA_HEADS) * (GLA_DK ** -0.5)
    k = split_heads(k, GLA_HEADS)
    v = split_heads(v, GLA_HEADS)
    lg_f = split_heads(jax.nn.log_sigmoid((a_f @ wa2_f + ba_f).astype(jnp.float32)) / GLA_GATE_TEMP, GLA_HEADS)
    lg_b = split_heads(jax.nn.log_sigmoid((a_b @ wa2_b + ba_b).astype(jnp.float32)) / GLA_GATE_TEMP, GLA_HEADS)
    o = bidir_scan(q, k, k, v, lg_f, lg_b)
    o = rms_norm(o, norm_w)
    return merge_heads(o) * jax.nn.silu(g)

def diff_branch(q, k, v, g, lq1, lk1, lq2, lk2, norm_w, lambda_init, pos):
    b_, l_, _ = q.shape
    q = q.reshape(b_, l_, DIFF_HEADS, 2, DIFF_HD).transpose(3, 0, 2, 1, 4)
    k = k.reshape(b_, l_, DIFF_HEADS, 2, DIFF_HD).transpose(3, 0, 2, 1, 4)
    q = rope(q, pos) * (DIFF_HD ** -0.5)
    k = rope(k, pos)
    v = split_heads(v, DIFF_HEADS)
    lam = (jnp.exp(jnp.sum(lq1 * lk1).astype(jnp.float32))
           - jnp.exp(jnp.sum(lq2 * lk2).astype(jnp.float32)) + lambda_init)
    nb = l_ // Q_BLOCK
    qb = jnp.moveaxis(q.reshape(2, b_, DIFF_HEADS, nb, Q_BLOCK, DIFF_HD), 3, 0)

    def block(qblk):
        s = jnp.einsum('cbhqd,cbhkd->cbhqk', qblk, k).astype(jnp.float32)
        p = jax.nn.softmax(s, axis=-1)
        w = p[0] - lam * p[1]
        return jnp.einsum('bhqk,bhkv->bhqv', w.astype(v.dtype), v)

    o = lax.map(block, qb)
    o = jnp.moveaxis(o, 0, 2).reshape(b_, DIFF_HEADS, l_, DIFF_DV)
    o = rms_norm(o, norm_w) * (1.0 - lambda_init)
    return merge_heads(o) * jax.nn.silu(g)

def hgrn_branch(q, z_f, z_b, i, g, lb, norm_w):
    lb32 = lb.astype(jnp.float32)

    def gates(z):
        z32 = z.astype(jnp.float32)
        one_minus_f = (1.0 - lb32) * jax.nn.sigmoid(-z32)
        f = lb32 + (1.0 - lb32) * jax.nn.sigmoid(z32)
        log_f = jnp.log(jnp.maximum(f, F_FLOOR))
        return split_heads(log_f, HGRN_HEADS), split_heads(one_minus_f.astype(z.dtype), HGRN_HEADS)

    lg_f, k_f = gates(z_f)
    lg_b, k_b = gates(z_b)
    o = bidir_scan(split_heads(q, HGRN_HEADS), k_f, k_b, split_heads(i, HGRN_HEADS), lg_f, lg_b)
    o = rms_norm(o, norm_w)
    return merge_heads(o) * jax.nn.silu(g)

def first_inputs(seed: int = 0) -> dict:
    key = jax.random.key(seed)
    ks = jax.random.split(key, 20)
    nrm = lambda k, shape, s: jax.random.normal(k, shape, jnp.float32) * s
    return {
        "x": nrm(ks[0], (BATCH, SEQ, D_MODEL), 1.0),
        "norm_pre": 1.0 + nrm(ks[1], (DEPTH, D_MODEL), 0.05),
        "norm_post": 1.0 + nrm(ks[2], (DEPTH, D_MODEL), 0.05),
        "w_in": nrm(ks[3], (DEPTH, D_MODEL, IN_W), D_MODEL ** -0.5),
        "w_out": nrm(ks[4], (DEPTH, MIX_W, D_MODEL), MIX_W ** -0.5),
        "gla_wa2_fwd": nrm(ks[5], (DEPTH, GLA_RANK, GLA_HEADS * GLA_DK), GLA_RANK ** -0.5),
        "gla_ba_fwd": nrm(ks[6], (DEPTH, GLA_HEADS * GLA_DK), 0.1),
        "gla_wa2_bwd": nrm(ks[7], (DEPTH, GLA_RANK, GLA_HEADS * GLA_DK), GLA_RANK ** -0.5),
        "gla_ba_bwd": nrm(ks[8], (DEPTH, GLA_HEADS * GLA_DK), 0.1),
        "gla_norm": 1.0 + nrm(ks[9], (DEPTH, GLA_DV), 0.05),
        "diff_lq1": nrm(ks[10], (DEPTH, DIFF_HD), 0.1),
        "diff_lk1": nrm(ks[11], (DEPTH, DIFF_HD), 0.1),
        "diff_lq2": nrm(ks[12], (DEPTH, DIFF_HD), 0.1),
        "diff_lk2": nrm(ks[13], (DEPTH, DIFF_HD), 0.1),
        "diff_norm": 1.0 + nrm(ks[14], (DEPTH, DIFF_DV), 0.05),
        "hgrn_lb_logits": nrm(ks[15], (DEPTH, HGRN_HEADS * HGRN_DK), 0.1),
        "hgrn_norm": 1.0 + nrm(ks[16], (DEPTH, HGRN_DV), 0.05),
    }

def first_block(x, norm_pre, norm_post, w_in, w_out, gla_wa2_fwd, gla_ba_fwd, gla_wa2_bwd, gla_ba_bwd,
              gla_norm, diff_lq1, diff_lk1, diff_lq2, diff_lk2, diff_norm, hgrn_lb_logits, hgrn_norm):
    pos = jnp.arange(x.shape[1], dtype=jnp.int32)
    p_lb = jax.nn.softmax(hgrn_lb_logits.astype(jnp.float32), axis=0)
    lb_all = jnp.cumsum(p_lb, axis=0) - p_lb[0:1]
    offs = _offsets()
    for layer in range(DEPTH):
        lambda_init = 0.8 - 0.6 * math.exp(-0.3 * layer)
        h = rms_norm(x, norm_pre[layer])
        proj = h @ w_in[layer]
        (gq, gk, gv, gg, gaf, gab, dq, dk, dv, dg, hq, hzf, hzb, hi, hg) = jnp.split(proj, offs, axis=-1)
        y_a = gla_branch(gq, gk, gv, gg, gaf, gab, gla_wa2_fwd[layer], gla_ba_fwd[layer],
                         gla_wa2_bwd[layer], gla_ba_bwd[layer], gla_norm[layer])
        y_b = diff_branch(dq, dk, dv, dg, diff_lq1[layer], diff_lk1[layer], diff_lq2[layer], diff_lk2[layer],
                          diff_norm[layer], lambda_init, pos)
        y_c = hgrn_branch(hq, hzf, hzb, hi, hg, lb_all[layer], hgrn_norm[layer])
        y = jnp.concatenate([y_a, y_b, y_c], axis=-1) @ w_out[layer]
        x = x + rms_norm(y, norm_post[layer])
    return x


DEPTH_2 = 1

GRID_W = 64
CTX_LEN = 256
NA_HEADS = 8
NA_HEAD_DIM = 64
NA_WIDTH = NA_HEADS * NA_HEAD_DIM
NA_KH = 8
NA_KW = 16
DN_HEADS = 8
DN_DK = 64
DN_DV = 64
DN_QK_W = DN_HEADS * DN_DK
DN_WIDTH = DN_HEADS * DN_DV
DN_CONV_W = 2 * DN_QK_W + DN_WIDTH
DN_CHUNK = 64
CONV_K = 3
ROPE_BASE = 10000.0
PROJ_WIDTH = 4 * NA_WIDTH + DN_CONV_W + DN_WIDTH + 4 * DN_HEADS + 2 * D_MODEL


def _rmsnorm(x, w):
    xf = x.astype(jnp.float32)
    y = xf * lax.rsqrt(jnp.mean(xf * xf, axis=-1, keepdims=True) + EPS)
    return (y * w.astype(jnp.float32)).astype(x.dtype)

def _l2norm(x):
    xf = x.astype(jnp.float32)
    return (xf * lax.rsqrt(jnp.sum(xf * xf, axis=-1, keepdims=True) + EPS)).astype(x.dtype)

def _heads(a, n_heads):
    return a.reshape(a.shape[:-1] + (n_heads, a.shape[-1] // n_heads))

def _rope_1d(x, pos):
    half = x.shape[-1] // 2
    freqs = ROPE_BASE ** (-jnp.arange(half, dtype=jnp.float32) / half)
    ang = pos.astype(jnp.float32)[:, None] * freqs[None, :]
    cos = jnp.concatenate([jnp.cos(ang), jnp.cos(ang)], -1)[None, :, None, :]
    sin = jnp.concatenate([jnp.sin(ang), jnp.sin(ang)], -1)[None, :, None, :]
    xf = x.astype(jnp.float32)
    rot = jnp.concatenate([-xf[..., half:], xf[..., :half]], -1)
    return (xf * cos + rot * sin).astype(x.dtype)

def _rope_2d(x, pos_row, pos_col):
    d = x.shape[-1] // 2
    return jnp.concatenate([_rope_1d(x[..., :d], pos_row), _rope_1d(x[..., d:], pos_col)], -1)

def _short_conv(x, w):
    return lax.conv_general_dilated(
        x, w.astype(x.dtype)[:, None, :], window_strides=(1,),
        padding=[(CONV_K // 2, CONV_K // 2)],
        dimension_numbers=('NWC', 'WIO', 'NWC'),
        feature_group_count=x.shape[-1])

def _split_proj(p):
    sizes = (NA_WIDTH, NA_WIDTH, NA_WIDTH, NA_WIDTH, DN_CONV_W, DN_WIDTH,
             2 * DN_HEADS, 2 * DN_HEADS, D_MODEL, D_MODEL)
    return jnp.split(p, np.cumsum(sizes)[:-1].tolist(), axis=-1)

def _na_latent(q, k, v, kc, vc, rpb):
    B, T, H, Dh = q.shape
    rows = T // GRID_W
    kh = min(NA_KH, rows)
    kg = k.reshape(B, rows, GRID_W, H, Dh)
    vg = v.reshape(B, rows, GRID_W, H, Dh)
    qg = q.reshape(B, rows, GRID_W, H, Dh)
    cq = jnp.arange(GRID_W)
    c0 = jnp.clip(cq - NA_KW // 2, 0, GRID_W - NA_KW)
    col_in = (cq[None, :] >= c0[:, None]) & (cq[None, :] < c0[:, None] + NA_KW)
    dx = jnp.clip(cq[None, :] - cq[:, None], -(NA_KW - 1), NA_KW - 1) + (NA_KW - 1)
    rpb_cols = rpb[:, :, dx]

    def row_step(args):
        r, q_r = args
        r0 = jnp.clip(r - kh // 2, 0, rows - kh)
        k_band = lax.dynamic_slice_in_dim(kg, r0, kh, axis=1)
        v_band = lax.dynamic_slice_in_dim(vg, r0, kh, axis=1)
        dy = r0 + jnp.arange(kh) - r + (NA_KH - 1)
        bias = jnp.take(rpb_cols, dy, axis=1).transpose(0, 2, 1, 3)
        s_win = jnp.einsum('bqhd,bywhd->bhqyw', q_r, k_band).astype(jnp.float32) + bias[None].astype(jnp.float32)
        s_win = jnp.where(col_in[:, None, :], s_win, -jnp.inf)
        s_ctx = jnp.einsum('bqhd,bchd->bhqc', q_r, kc).astype(jnp.float32)
        s = jnp.concatenate([s_win.reshape(B, H, GRID_W, kh * GRID_W), s_ctx], axis=-1)
        pr = jax.nn.softmax(s, axis=-1).astype(v.dtype)
        p_win = pr[..., :kh * GRID_W].reshape(B, H, GRID_W, kh, GRID_W)
        p_ctx = pr[..., kh * GRID_W:]
        return (jnp.einsum('bhqyw,bywhd->bqhd', p_win, v_band)
                + jnp.einsum('bhqc,bchd->bqhd', p_ctx, vc))

    o = lax.map(row_step, (jnp.arange(rows), jnp.moveaxis(qg, 1, 0)))
    return jnp.moveaxis(o, 0, 1).reshape(B, T, H, Dh)

def _dense_attention(q, k, v):
    s = jnp.einsum('bqhd,bkhd->bhqk', q, k).astype(jnp.float32)
    p = jax.nn.softmax(s, axis=-1).astype(v.dtype)
    return jnp.einsum('bhqk,bkhd->bqhd', p, v)

def _gdn_chunked(q, k, v, g, beta, s0):
    out_dtype = v.dtype
    f32 = jnp.float32
    B, T, H, DK = q.shape
    DV = v.shape[-1]
    C = DN_CHUNK
    N = T // C

    def blk(a):
        a = a.astype(f32).reshape((B, N, C, H) + a.shape[3:])
        return jnp.swapaxes(a, 2, 3)

    q, k, v, g, beta = blk(q), blk(k), blk(v), blk(g), blk(beta)
    gc = jnp.cumsum(g, axis=-1)
    incl = jnp.tril(jnp.ones((C, C), bool))
    strict = jnp.tril(jnp.ones((C, C), bool), -1)
    decay = jnp.exp(jnp.where(incl, gc[..., :, None] - gc[..., None, :], -jnp.inf))
    kb = k * beta[..., None]
    lower = jnp.where(strict, jnp.einsum('bnhid,bnhjd->bnhij', kb, k) * decay, 0.0)
    a_mat = lower + jnp.eye(C, dtype=f32)
    rhs = jnp.concatenate([v * beta[..., None], kb * jnp.exp(gc)[..., None]], axis=-1)
    sol = lax.linalg.triangular_solve(a_mat, rhs, left_side=True, lower=True, unit_diagonal=True)
    u, wk = sol[..., :DV], sol[..., DV:]
    qk = jnp.einsum('bnhid,bnhjd->bnhij', q, k) * decay
    q_dec = q * jnp.exp(gc)[..., None]
    k_dec = k * jnp.exp(gc[..., -1:] - gc)[..., None]
    g_tot = jnp.exp(gc[..., -1])

    def step(S, xs):
        qk_i, qd_i, kd_i, u_i, w_i, gt_i = xs
        v_new = u_i - jnp.einsum('bhck,bhkv->bhcv', w_i, S)
        o_i = jnp.einsum('bhck,bhkv->bhcv', qd_i, S) + jnp.einsum('bhij,bhjv->bhiv', qk_i, v_new)
        S = S * gt_i[..., None, None] + jnp.einsum('bhck,bhcv->bhkv', kd_i, v_new)
        return S, o_i

    xs = (jnp.moveaxis(qk, 1, 0), jnp.moveaxis(q_dec, 1, 0), jnp.moveaxis(k_dec, 1, 0),
          jnp.moveaxis(u, 1, 0), jnp.moveaxis(wk, 1, 0), jnp.moveaxis(g_tot, 1, 0))
    s_fin, o = lax.scan(step, s0.astype(f32), xs)
    o = jnp.transpose(o, (1, 0, 3, 2, 4)).reshape(B, T, H, DV)
    return o.astype(out_dtype), s_fin

def _dn_prepare(qkv_raw, b_raw, a_raw, w, pos):
    B, T, _ = qkv_raw.shape
    f32 = jnp.float32
    qkv = jax.nn.silu(_short_conv(qkv_raw, w['conv_w']))
    q, k, v = jnp.split(qkv, [DN_QK_W, 2 * DN_QK_W], axis=-1)
    q = _l2norm(_heads(q, DN_HEADS))
    k = _l2norm(_heads(k, DN_HEADS))
    v = _heads(v, DN_HEADS)
    if pos is not None:
        q = _rope_2d(q, pos[0], pos[1])
        k = _rope_2d(k, pos[0], pos[1])
    q = q * DN_DK ** -0.5
    beta = jax.nn.sigmoid(b_raw.astype(f32)).reshape(B, T, 2, DN_HEADS)
    g = -jnp.exp(w['dn_A_log'].astype(f32)) * jax.nn.softplus(
        a_raw.astype(f32).reshape(B, T, 2, DN_HEADS) + w['dn_dt_bias'].astype(f32))
    return q, k, v, beta, g

def _bidir_delta(q, k, v, beta, g, s0_f, s0_b):
    rev = lambda a: jnp.flip(a, axis=1)
    o_f, s_f = _gdn_chunked(q, k, v, g[:, :, 0], beta[:, :, 0], s0_f)
    o_b, s_b = _gdn_chunked(rev(q), rev(k), rev(v), rev(g[:, :, 1]), rev(beta[:, :, 1]), s0_b)
    return o_f + rev(o_b), s_f, s_b

def _merge(o_na, z_na, o_dn, z_dn, g_na, g_dn, w):
    B, T = o_na.shape[:2]
    u_na = (o_na.reshape(B, T, NA_WIDTH) * jax.nn.silu(z_na)) @ w['w_o_na']
    o_dn = _rmsnorm(o_dn, w['dn_norm_w']).reshape(B, T, DN_WIDTH)
    u_dn = (o_dn * jax.nn.silu(z_dn)) @ w['w_o_dn']
    y = jax.nn.sigmoid(g_na) * u_na + jax.nn.sigmoid(g_dn) * u_dn
    return y @ w['w_out']

def _layer(x, ctx, c, c_ctx, w, last):
    B, T, _ = x.shape
    t = jnp.arange(T)
    pos = (t // GRID_W, t % GRID_W)
    shift, scale, gate = jnp.split(jax.nn.silu(c) @ w['mod_w'] + w['mod_b'], 3, axis=-1)
    shift_c, scale_c, gate_c = jnp.split(jax.nn.silu(c_ctx) @ w['mod_w'] + w['mod_b'], 3, axis=-1)
    h = _rmsnorm(x, w['norm_w']) * (1.0 + scale[:, None]) + shift[:, None]
    hc = _rmsnorm(ctx, w['norm_w']) * (1.0 + scale_c) + shift_c
    na_q, na_k, na_v, na_z, dn_qkv, dn_z, dn_b, dn_a, g_na, g_dn = _split_proj(h @ w['w_in'])
    na_qc, na_kc, na_vc, na_zc, dn_qkvc, dn_zc, dn_bc, dn_ac, g_nac, g_dnc = _split_proj(hc @ w['w_in'])

    q = _rmsnorm(_heads(na_q, NA_HEADS), w['na_q_norm']) * NA_HEAD_DIM ** -0.5
    k = _rmsnorm(_heads(na_k, NA_HEADS), w['na_k_norm'])
    v = _heads(na_v, NA_HEADS)
    kc = _rmsnorm(_heads(na_kc, NA_HEADS), w['na_k_norm'])
    vc = _heads(na_vc, NA_HEADS)
    o_na = _na_latent(q, k, v, kc, vc, w['na_rpb'])

    dq, dk, dv, dbeta, dg = _dn_prepare(dn_qkv, dn_b, dn_a, w, pos)
    dqc, dkc, dvc, dbetac, dgc = _dn_prepare(dn_qkvc, dn_bc, dn_ac, w, None)
    zeros = jnp.zeros((ctx.shape[0], DN_HEADS, DN_DK, DN_DV), jnp.float32)
    o_dnc, s_f, s_b = _bidir_delta(dqc, dkc, dvc, dbetac, dgc, zeros, zeros)
    o_dn, _, _ = _bidir_delta(dq, dk, dv, dbeta, dg, s_f, s_b)

    x = x + gate[:, None] * _merge(o_na, na_z, o_dn, dn_z, g_na, g_dn, w)
    if not last:
        qc = _rmsnorm(_heads(na_qc, NA_HEADS), w['na_q_norm']) * NA_HEAD_DIM ** -0.5
        o_nac = _dense_attention(qc, kc, vc)
        ctx = ctx + gate_c * _merge(o_nac, na_zc, o_dnc, dn_zc, g_nac, g_dnc, w)
    return x, ctx

def second_inputs(seed: int = 0) -> dict:
    key = jax.random.key(seed)
    ks = jax.random.split(key, 20)
    f32 = jnp.float32

    def nrm(k, shape, s):
        return jax.random.normal(k, shape, f32) * s

    x = nrm(ks[0], (BATCH, SEQ, D_MODEL), 1.0)
    c = nrm(ks[1], (BATCH, D_MODEL), 1.0)
    ctx = nrm(ks[2], (BATCH, CTX_LEN, D_MODEL), 1.0)
    c_ctx = nrm(ks[3], (D_MODEL,), 1.0)
    mod_w = nrm(ks[4], (DEPTH_2, D_MODEL, 3 * D_MODEL), 0.5 * D_MODEL ** -0.5)
    mod_b = nrm(ks[5], (DEPTH_2, 3 * D_MODEL), 0.01)
    norm_w = 1.0 + nrm(ks[6], (DEPTH_2, D_MODEL), 0.01)
    w_in = nrm(ks[7], (DEPTH_2, D_MODEL, PROJ_WIDTH), D_MODEL ** -0.5)
    conv_w = nrm(ks[8], (DEPTH_2, CONV_K, DN_CONV_W), CONV_K ** -0.5)
    na_q_norm = 1.0 + nrm(ks[9], (DEPTH_2, NA_HEAD_DIM), 0.01)
    na_k_norm = 1.0 + nrm(ks[10], (DEPTH_2, NA_HEAD_DIM), 0.01)
    na_rpb = nrm(ks[11], (DEPTH_2, NA_HEADS, 2 * NA_KH - 1, 2 * NA_KW - 1), 0.1)
    dn_A_log = jnp.log(jax.random.uniform(ks[12], (DEPTH_2, 2, DN_HEADS), f32, 1.0, 16.0))
    dt = jnp.exp(jax.random.uniform(ks[13], (DEPTH_2, 2, DN_HEADS), f32, math.log(1e-3), math.log(1e-1)))
    dn_dt_bias = dt + jnp.log(-jnp.expm1(-dt))
    dn_norm_w = 1.0 + nrm(ks[14], (DEPTH_2, DN_DV), 0.01)
    w_o_na = nrm(ks[15], (DEPTH_2, NA_WIDTH, D_MODEL), NA_WIDTH ** -0.5)
    w_o_dn = nrm(ks[16], (DEPTH_2, DN_WIDTH, D_MODEL), DN_WIDTH ** -0.5)
    w_out = nrm(ks[17], (DEPTH_2, D_MODEL, D_MODEL), D_MODEL ** -0.5)
    return {'x': x, 'c': c, 'ctx': ctx, 'c_ctx': c_ctx, 'mod_w': mod_w, 'mod_b': mod_b,
            'norm_w': norm_w, 'w_in': w_in, 'conv_w': conv_w, 'na_q_norm': na_q_norm,
            'na_k_norm': na_k_norm, 'na_rpb': na_rpb, 'dn_A_log': dn_A_log, 'dn_dt_bias': dn_dt_bias,
            'dn_norm_w': dn_norm_w, 'w_o_na': w_o_na, 'w_o_dn': w_o_dn, 'w_out': w_out}

def second_block(x, c, ctx, c_ctx, mod_w, mod_b, norm_w, w_in, conv_w, na_q_norm, na_k_norm, na_rpb,
              dn_A_log, dn_dt_bias, dn_norm_w, w_o_na, w_o_dn, w_out):
    for l in range(DEPTH_2):
        w = {'mod_w': mod_w[l], 'mod_b': mod_b[l], 'norm_w': norm_w[l], 'w_in': w_in[l],
             'conv_w': conv_w[l], 'na_q_norm': na_q_norm[l], 'na_k_norm': na_k_norm[l],
             'na_rpb': na_rpb[l], 'dn_A_log': dn_A_log[l], 'dn_dt_bias': dn_dt_bias[l],
             'dn_norm_w': dn_norm_w[l], 'w_o_na': w_o_na[l], 'w_o_dn': w_o_dn[l], 'w_out': w_out[l]}
        x, ctx = _layer(x, ctx, c, c_ctx, w, l == DEPTH_2 - 1)
    return x


def setup_inputs(seed=0):
    out = dict(first_inputs(seed))
    for name, value in second_inputs(seed + 1).items():
        if name != "x":
            out[name + "_2"] = value
    return out


def reference(
    x, norm_pre, norm_post, w_in, w_out, gla_wa2_fwd, gla_ba_fwd, gla_wa2_bwd, gla_ba_bwd,
    gla_norm, diff_lq1, diff_lk1, diff_lq2, diff_lk2, diff_norm, hgrn_lb_logits, hgrn_norm, c_2,
    ctx_2, c_ctx_2, mod_w_2, mod_b_2, norm_w_2, w_in_2, conv_w_2, na_q_norm_2, na_k_norm_2,
    na_rpb_2, dn_A_log_2, dn_dt_bias_2, dn_norm_w_2, w_o_na_2, w_o_dn_2, w_out_2,
):
    x = first_block(
        x, norm_pre, norm_post, w_in, w_out, gla_wa2_fwd, gla_ba_fwd, gla_wa2_bwd, gla_ba_bwd,
        gla_norm, diff_lq1, diff_lk1, diff_lq2, diff_lk2, diff_norm, hgrn_lb_logits, hgrn_norm,
    )
    return second_block(
        x, c_2, ctx_2, c_ctx_2, mod_w_2, mod_b_2, norm_w_2, w_in_2, conv_w_2, na_q_norm_2,
        na_k_norm_2, na_rpb_2, dn_A_log_2, dn_dt_bias_2, dn_norm_w_2, w_o_na_2, w_o_dn_2,
        w_out_2,
    )


_drawn_inputs = setup_inputs


def setup_inputs(seed=0):
    import zlib

    import numpy as np

    out = dict(_drawn_inputs(seed))
    spreads = {}
    factors = {'gla_ba_fwd': 2.727,
     'gla_ba_bwd': 2.929,
     'ctx_2': 8.0,
     'c_ctx_2': 4.718,
     'mod_b_2': 8.0,
     'norm_w_2': 8.0,
     'na_q_norm_2': 8.0,
     'na_k_norm_2': 8.0,
     'na_rpb_2': 8.0,
     'dn_A_log_2': 5.317,
     'dn_norm_w_2': 8.0,
     'w_o_na_2': 3.209}
    for name, (base, spread) in spreads.items():
        noise = np.random.default_rng([zlib.crc32(name.encode()), seed]).standard_normal(out[name].shape)
        drawn = base * np.exp(spread * noise) if base else spread * noise
        out[name] = jnp.asarray(drawn.astype(out[name].dtype))
    for name, factor in factors.items():
        out[name] = (out[name] * factor).astype(out[name].dtype)
    return out
```

```python
from contextlib import ExitStack, contextmanager
import math

import numpy as np
import concourse.bass as bass
from concourse import mybir

F32 = mybir.dt.float32
U32 = mybir.dt.uint32
ALU = mybir.AluOpType
ACT = mybir.ActivationFunctionType
AX = mybir.AxisListType.X
P = 128
D = 1024
T = 1024
NT = T // P
KT = D // P
EPS = 1e-6

DEPTH = 2
W1 = 4128
GQ, GK, GV, GG, GA = 0, 128, 256, 512, 768
DQ, DK, DV, DG = 800, 1312, 1824, 2336
HQ, HZ, HI, HG = 2848, 3104, 3616, 3872
LEVELS = 7
CTX = 256
T2 = T + CTX
NT2 = T2 // P
NCTX = CTX // P
NK, NV, CONV, BETA, GATE, NQ, NZ, DZ, GNA, GDN = 0, 512, 1024, 2560, 2576, 2592, 3104, 3616, 4128, 5152
W2 = 6176
BOTH = NQ


class Mark:

    def __init__(self, sem, value):
        self.sem, self.value = sem, value


def after(engine, *marks, apart=None):
    for mark in marks or [None]:
        if mark is not None and mark.sem is not None:
            engine.wait_ge(mark.sem, mark.value)
        if apart is not None:
            engine.sem_inc(apart, 1)


class Book:

    def __init__(self):
        self.per, self.named, self.most = {}, {}, {}


class Counter:

    def __init__(self, kit, name, step=1):
        self.kit, self.name, self.step = kit, name, step
        self.sem = kit.sem(name)
        self.base = self.n = 0
        kit.counters.append(self)

    def done(self, instruction, name=None):
        instruction.then_inc(self.sem, self.step)
        self.n += self.step
        if name:
            self.kit.new.named[self.kit.stage_name, self.name, name] = self.n
        return Mark(self.sem, self.base + self.n)

    def last(self, name):
        key = (self.kit.stage_name, self.name)
        if (*key, name) not in self.kit.old.named:
            return Mark(None, 0)
        return Mark(self.sem, self.base + (self.kit.old.named[(*key, name)] - self.kit.old.per[key]))


class Kit:
    def __init__(self, nc, ctx, old):
        self.nc, self.ctx, self.old, self.new = nc, ctx, old, Book()
        self.counters = []
        self.stage_name = ""

    def sem(self, name):
        return self.ctx.enter_context(self.nc.semaphore(name))

    def stage(self, name):
        nc = self.nc
        self.stage_name = name
        nc.all_engine_barrier()
        for c in self.counters:
            nc.gpsimd.sem_clear(c.sem)
            c.base, c.n = 0, self.old.per.get((name, c.name), 0)
            if c.n:
                nc.gpsimd.sem_inc(c.sem, c.n)
        nc.all_engine_barrier()

    @contextmanager
    def rounds(self, n):
        start = [c.n for c in self.counters]
        with self.nc.Fori(0, n) as i:
            for c, s in zip(self.counters, start):
                per = self.old.per.get((self.stage_name, c.name), 0)
                c.base, c.n = (i * per + s if per else s), 0
            yield i
            got = [c.n for c in self.counters]
        for c, s, g in zip(self.counters, start, got):
            self.new.per[self.stage_name, c.name] = g
            c.base, c.n = 0, s + n * g


def constants():
    f = np.float32
    i = np.arange(P)
    out = {"c_ident": np.eye(P, dtype=f)}
    pos = np.arange(T, dtype=f)
    ang = pos[:, None] * (f(10000.0) ** (-np.arange(0, 64, 2, dtype=f) / f(64)))[None, :]
    out["c_rope1"] = np.concatenate([np.cos(ang), np.sin(ang)], 1).astype(f)
    fr = f(10000.0) ** (-np.arange(16, dtype=f) / f(16))
    t = np.arange(T)
    row, col = (t // 64).astype(f)[:, None] * fr, (t % 64).astype(f)[:, None] * fr
    out["c_rope2"] = np.stack([np.cos(row), np.cos(col), np.sin(row), np.sin(col)], 1).reshape(T, 64).astype(f)
    m = [np.eye(P)]
    for b in range(1, LEVELS + 1):
        same = (i[:, None] >> b) == (i[None, :] >> b)
        m.append(same & ((i[:, None] >> (b - 1)) != (i[None, :] >> (b - 1))))
    out["c_levels"] = np.stack(m, 1).astype(f)
    bd = np.zeros((P, 512), f)
    for h in range(4):
        bd[32 * h:32 * h + 32, 64 * h:64 * h + 64] = 1
        bd[64 * (h % 2):64 * (h % 2) + 64, 256 + 64 * h:256 + 64 * h + 64] = 1
    out["c_heads"] = bd
    out["c_layers"] = np.stack([np.array([0.0, 1.0]), np.array([0.8 - 0.6 * math.exp(-0.3 * l) for l in range(DEPTH)]),
                                np.array([1.0 - (0.8 - 0.6 * math.exp(-0.3 * l)) for l in range(DEPTH)])], 1).astype(f)
    r = np.arange(64)
    k, c = r[:, None], r[None, :]
    z = np.zeros((64, 64))
    both = lambda a, b: np.block([[a, z], [z, b]])
    upto = np.concatenate([k <= c, k >= c], 0)
    mats = [both(k > c, k < c), both(k <= c, k >= c), both(z + 1, z + 1)]
    out["c_sums"] = np.stack(mats, 1).astype(f)
    lv = [upto]
    for b in range(1, 7):
        blk = ((k >> b) == (c >> b)) & ((k >> (b - 1)) != (c >> (b - 1)))
        lv.append(np.concatenate([blk & (k < c), blk & (k > c)], 0))
    lv.append(np.concatenate([k == c, k == c], 0))
    out["c_tri"] = np.stack(lv, 1).astype(f)
    c0 = np.clip(r - 8, 0, 48)[:, None]
    out["c_cols"] = np.where((c >= c0) & (c < c0 + 16), 0, -1e30).astype(f)
    rows = np.zeros((P, 10), f)
    rows[:64, 8:] = -1e30
    rows[64:, 0] = rows[64:, 9] = -1e30
    out["c_rows"] = rows
    return out


def bc(ap, shape):
    return ap.broadcast_to(shape)


class Program:
    def __init__(self, nc, args, out, old):
        self.nc, self.a, self.out = nc, args, out
        self.ctx = ExitStack()
        self.old = old

    def dram(self, name, shape):
        return self.nc.dram_tensor(name, shape, F32, kind="Internal").ap()

    def build(self, upto=99):
        nc = self.nc
        with self.ctx:
            self.kit = k = Kit(nc, self.ctx, self.old)
            self.pe, self.dve, self.act, self.pool = (Counter(k, n) for n in ("pe", "dve", "act", "pool"))
            self.load = [Counter(k, f"load{i}", 16) for i in range(8)]
            self.store = [Counter(k, f"store{i}", 16) for i in range(8)]
            self.aside = k.sem("aside")
            self.psum = self.ctx.enter_context(nc.psum_tensor("psum", [P, 8, 512], F32))
            self.ident = self.ctx.enter_context(nc.sbuf_tensor("ident", [P, P], F32))
            self.xs = self.dram("x_stream", [T, D])
            self.p1 = self.dram("proj1", [T, W1])
            self.o_scan = self.dram("o_scan", [T, 512])
            self.o_diff = self.dram("o_diff", [T, 512])
            self.qk_t = self.dram("qk_t", [2, 4, P, T])
            k.stage("start")
            a = self.load[0].done(nc.sync.dma_start(self.ident[:], self.a["c_ident"]))
            b = self.load[1].done(nc.sync.dma_start(self.xs, self.a["x"].rearrange("a t d -> (a t) d")))
            after(nc.sync, a, b)
            with nc.Fori(0, DEPTH) as layer:
                with self.sb("h_t", [P, KT, T]) as h_t:
                    self.norm("norm1", self.xs, NT, h_t, 0, self.a["norm_pre"][bass.ds(layer, 1), :])
                    self.project("proj1", h_t, NT, self.a["w_in"][bass.ds(layer, 1)].rearrange("a k n -> (a k) n"),
                                 12, 344, self.p1)
                if upto > 1:
                    self.scan_branches(layer)
                if upto > 2:
                    self.diff_prepare()
                    self.diff_attention(layer)
                if upto > 3:
                    self.merge1(layer)
            if upto > 4:
                self.block2(upto)
            k.stage("end")
        return k.new

    @contextmanager
    def sb(self, name, shape):
        with self.nc.sbuf_tensor(f"{name}_{self.nc.next_id()}", shape, F32) as t:
            yield t

    def buffers(self, stack, *shapes):
        return [stack.enter_context(self.sb(f"buffer{n}", shape)) for n, shape in enumerate(shapes)]

    def chain(self, counter, instruction):
        m = counter.done(instruction)
        after({"dve": self.nc.vector, "act": self.nc.scalar, "pool": self.nc.gpsimd, "pe": self.nc.tensor}[counter.name], m)
        return m

    def rstd(self, ms, out, scale):
        nc = self.nc
        m = self.dve.done(nc.vector.tensor_scalar(ms, ms, scale, EPS, ALU.mult, ALU.add))
        after(nc.scalar, m)
        self.chain(self.act, nc.scalar.activation(out, ms, ACT.Ln))
        return self.act.done(nc.scalar.activation(out, out, ACT.Exp, scale=-0.5))

    @staticmethod
    def row2(tile):
        return 1 + tile * P + (tile >= NCTX)

    def norm(self, name, src, n, out, first, weight, shift=None):
        nc, k, ps = self.nc, self.kit, self.psum
        k.stage(name)
        with ExitStack() as st:
            x, xn, w, b, ss, rs = self.buffers(st, [P, 2, D], [P, 2, D], [P, D], [P, D], [P, 2], [P, 2])
            wl = self.load[2].done(nc.sync.dma_start(w[:], weight.partition_broadcast(P) if len(weight.shape) == 1 else bc(weight, [P, D])))
            after(nc.vector, wl)
            if shift is not None:
                bl = self.load[3].done(nc.sync.dma_start(b[:], bc(shift, [P, D])))
                after(nc.vector, bl)
            with k.rounds(n // 2) as i:
                for s in range(2):
                    after(nc.sync, self.dve.last(f"normed{s}"), apart=self.aside)
                    xl = self.load[s].done(nc.sync.dma_start(x[:, s, :], src[bass.ds(i * 2 * P + s * P, P), :]))
                    after(nc.scalar, xl, self.pe.last(f"transposed{s}"))
                    sq = self.act.done(nc.scalar.activation(xn[:, s, :], x[:, s, :], ACT.Square, accum_out=ss[:, s:s + 1]))
                    after(nc.vector, sq)
                    r = self.rstd(ss[:, s:s + 1], rs[:, s:s + 1], 1.0 / D)
                    after(nc.vector, r)
                    m = self.dve.done(nc.vector.scalar_tensor_tensor(out=xn[:, s, :], in0=x[:, s, :], scalar=rs[:, s:s + 1],
                                                                     in1=w[:], op0=ALU.mult, op1=ALU.mult), f"normed{s}")
                    if shift is not None:
                        after(nc.vector, m)
                        m = self.dve.done(nc.vector.tensor_tensor(xn[:, s, :], xn[:, s, :], b[:], ALU.add))
                    after(nc.tensor, m, self.act.last(f"out{s}"), self.dve.last(f"out{s}"))
                    for kt in range(KT):
                        ins = nc.tensor.transpose(ps[:, 2 * s + kt // 4, kt % 4 * P:kt % 4 * P + P], xn[:, s, kt * P:kt * P + P], self.ident[:])
                    tr = self.pe.done(ins, f"transposed{s}")
                    col = bass.ds(i * 2 * P + (first + s * P), P)
                    src_ps = lambda b: ps[:, 2 * s + b, :].rearrange("p (k t) -> p k t", k=4)
                    after(nc.scalar, tr)
                    self.act.done(nc.scalar.activation(out[:, 0:4, col], src_ps(0), ACT.Copy), f"out{s}")
                    after(nc.vector, tr)
                    self.dve.done(nc.vector.tensor_copy(out[:, 4:8, col], src_ps(1)), f"out{s}")

    def project(self, name, h_t, n_tok, w, n_cols, width, dst, col0=0, tok0=0, row_of=lambda t: t * P):
        nc, k, ps = self.nc, self.kit, self.psum
        k.stage(name)
        with ExitStack() as st:
            wt, y = self.buffers(st, [P, 2, KT, width], [P, 4, width])
            with k.rounds(n_cols // 2) as i:
                for s in range(2):
                    cols = bass.ds(i * 2 * width + (col0 + s * width), width)
                    after(nc.sync, self.pe.last(f"used{s}"), apart=self.aside)
                    wl = self.load[s].done(nc.sync.dma_start(wt[:, s], w[:, cols].rearrange("(k p) n -> p k n", p=P)))
                    after(nc.tensor, wl)
                    for t in range(n_tok):
                        j = s * n_tok + t
                        bank, turn = j % 4, (j // 4) % 2
                        c, eng = ((self.act, nc.scalar), (self.dve, nc.vector))[bank % 2]
                        after(nc.tensor, out_marks[j - 4] if j >= 4 else c.last(f"copied{2 * n_tok - 4 + j}"))
                        for kt in range(KT):
                            ins = nc.tensor.matmul(ps[:, bank, 0:width], h_t[:, kt, (tok0 + t) * P:(tok0 + t + 1) * P], wt[:, s, kt, :],
                                                   start=kt == 0, stop=kt == KT - 1)
                        mm = self.pe.done(ins, f"used{s}" if t == n_tok - 1 else None)
                        if j == 0:
                            out_marks, kept = {}, {}
                        after(eng, mm, kept[j - 4] if j >= 4 else self.store[bank].last(f"kept{2 * n_tok - 4 + j}"))
                        if bank % 2 == 0:
                            cp = nc.scalar.activation(y[:, bank, :], ps[:, bank, 0:width], ACT.Copy)
                        else:
                            cp = nc.vector.tensor_copy(y[:, bank, :], ps[:, bank, 0:width])
                        out_marks[j] = c.done(cp, f"copied{j}")
                        after(nc.scalar, out_marks[j])
                        kept[j] = self.store[bank].done(nc.scalar.dma_start(
                            dst[row_of(tok0 + t):row_of(tok0 + t) + P, cols],
                            y[:, bank, :]), f"kept{j}")
            for b in range(4):
                after(nc.scalar, Mark(self.store[b].sem, self.store[b].n))

    def scan_branches(self, layer):
        nc, k, ps = self.nc, self.kit, self.psum
        with ExitStack() as outer:
            qd, u, gt, o = self.buffers(outer, [P, NT, 2, 3, P], [P, NT, 2, 512], [P, NT, 2, 3], [P, NT, 512])
            self.scan_chunks(layer, qd, u, gt, o)
            self.scan_states(qd, u, gt, o)

    def scan_chunks(self, layer, qd, u, gt, o):
        nc, k, ps = self.nc, self.kit, self.psum
        V, S, G, PE = nc.vector, nc.scalar, nc.gpsimd, nc.tensor
        k.stage("scan")
        with ExitStack() as st:
            (nat, lmask, heads, wa, ba, lbl, lb, oml, lbt, one, at, lt, kt, qt, lg, b, z, e, sg, f1, f2, kd, kn, am, mk, mq, d) = self.buffers(
                st, [P, 1568], [P, 8, P], [P, 512], [16, 2, P], [P, 2], [P, 2, 2], [P, 2], [P, 2],
                [P, 4], [P, P], [16, 2, P], [P, 2, P], [P, 2, 3, P], [P, 3, P], [P, 2, 3, P], [P, 2, 3, P],
                [P, 512], [P, 2, 512], [P, 2, 512], [P, 512], [P, 512], [P, 2, 3, P], [P, 2, 384],
                [P, 2, 512], [P, 8, 3, P], [P, 8, 3, P], [P, 2, 2, 3, P])
            ld = []
            a = self.a
            for i, (dst, src) in enumerate([(lmask[:], a["c_levels"]), (heads[:], a["c_heads"]),
                                            (wa[:, 0, :], a["gla_wa2_fwd"][bass.ds(layer, 1)].rearrange("a k n -> (a k) n")),
                                            (wa[:, 1, :], a["gla_wa2_bwd"][bass.ds(layer, 1)].rearrange("a k n -> (a k) n")),
                                            (ba[:, 0:1], a["gla_ba_fwd"][bass.ds(layer, 1), :].rearrange("a p -> p a")),
                                            (ba[:, 1:2], a["gla_ba_bwd"][bass.ds(layer, 1), :].rearrange("a p -> p a")),
                                            (lbt[:, 3:4], bc(a["c_layers"][bass.ds(layer, 1), 0:1], [P, 1]))]):
                with nc.allow_non_contiguous_dma(reason="one value per partition"):
                    ld.append(self.load[1 + i].done(nc.sync.dma_start(dst, src)))
            with nc.allow_non_contiguous_dma(reason="one value per partition"):
                m = self.load[0].done(nc.sync.dma_start(lbl[:].rearrange("p l t -> p (l t)"), a["hgrn_lb_logits"].rearrange("l (t p) -> p (l t)", p=P)))
            ld.append(m)
            after(V, *ld)
            after(PE, *ld)
            after(nc.sync, *ld)
            c = lambda ins: self.chain(self.dve, ins)
            c(V.memset(one[:], 1.0))
            c(V.tensor_tensor(lbt[:, 0:2], lbl[:, 0, :], lbl[:, 1, :], ALU.max))
            m = c(V.tensor_tensor(lbl[:], lbl[:], bc(lbt[:, 0:2].unsqueeze(1), [P, 2, 2]), ALU.subtract))
            after(S, m)
            m = self.act.done(S.activation(lbl[:], lbl[:], ACT.Exp))
            after(V, m)
            c(V.tensor_tensor(lb[:], lbl[:, 0, :], lbl[:, 1, :], ALU.add))
            c(V.reciprocal(lb[:], lb[:]))
            c(V.tensor_tensor(lb[:], lb[:], lbl[:, 1, :], ALU.mult))
            c(V.tensor_scalar(lb[:], lb[:], lbt[:, 3:4], None, ALU.mult))
            ready = c(V.tensor_scalar(oml[:], lb[:], -1.0, 1.0, ALU.mult, ALU.add))
            with k.rounds(NT) as i:
                after(nc.sync, self.pe.last("nat"), apart=self.aside)
                rows = self.p1[bass.ds(i * P, P)]
                l0 = self.load[0].done(nc.sync.dma_start(nat[:, 0:512], rows[:, 0:512]))
                l1 = self.load[1].done(nc.sync.dma_start(nat[:, 512:544], rows[:, GA:GA + 32]))
                l2 = self.load[2].done(nc.sync.dma_start(nat[:, 544:1568], rows[:, HQ:HQ + 1024]))
                after(PE, l0, l1, l2, self.dve.last("a_done"), self.act.last("o_copied"))
                for j, col in enumerate((0, 544, 672, 128)):
                    PE.transpose(ps[:, 0, j * P:j * P + P], nat[:, col:col + P], self.ident[:])
                for j in range(4):
                    PE.transpose(ps[:, 1, j * P:j * P + P], nat[:, 800 + j * P:928 + j * P], self.ident[:])
                for j in range(2):
                    ins = PE.transpose(ps[0:16, 2, j * P:j * P + P], nat[:, 512 + 16 * j:528 + 16 * j], self.ident[:])
                tr = self.pe.done(ins)
                after(S, tr, self.pe.last("logits"), self.pool.last("mixed"), self.dve.last("mixed"), self.dve.last("kd"))
                ca = self.act.done(S.activation(at[:], ps[0:16, 2, 0:256].rearrange("p (j t) -> p j t", j=2), ACT.Copy))
                self.act.done(S.activation(qt[:, 0, :], ps[:, 0, 0:P], ACT.Copy, scale=32 ** -0.5))
                self.act.done(S.activation(qt[:, 1:3, :], ps[:, 0, P:3 * P].rearrange("p (j t) -> p j t", j=2), ACT.Copy))
                cq = self.act.done(S.activation(kt[:, :, 0, :], bc(ps[:, 0, 3 * P:4 * P].unsqueeze(1), [P, 2, P]), ACT.Copy))
                after(PE, ca)
                for j in range(2):
                    ins = PE.matmul(ps[:, 2, 256 + j * P:256 + (j + 1) * P], wa[:, j, :], at[:, j, :], start=True, stop=True)
                lo = self.pe.done(ins, "logits")
                after(V, lo)
                for j in range(2):
                    m = self.dve.done(V.tensor_scalar(lt[:, j, :], ps[:, 2, 256 + j * P:256 + (j + 1) * P], ba[:, j:j + 1], None, ALU.add))
                after(V, m)
                m2 = self.dve.done(V.tensor_scalar(z[:], ps[:, 1, :], -87.0, 87.0, ALU.max, ALU.min))
                after(S, m, m2)
                self.chain(self.act, S.activation(f1[:, 0:256], lt[:].rearrange("p j t -> p (j t)"), ACT.Abs))
                xa = self.chain(self.act, S.activation(f1[:, 0:256], f1[:, 0:256], ACT.Exp, scale=-1.0))
                x1 = self.act.done(S.activation(f1[:, 0:256], f1[:, 0:256], ACT.Ln, bias=1.0))
                self.act.done(S.activation(e[:, 0, :], z[:], ACT.Exp, scale=-1.0))
                x2 = self.act.done(S.activation(e[:, 1, :], z[:], ACT.Exp))
                after(V, xa)
                c(V.tensor_scalar(lt[:], lt[:], 0.0, None, ALU.min))
                after(V, x1)
                c(V.tensor_tensor(lt[:], lt[:], f1[:, 0:256].rearrange("p (j t) -> p j t", j=2), ALU.subtract))
                self.dve.done(V.tensor_scalar(lg[:, :, 0, :], lt[:], 1.0 / 16.0, None, ALU.mult))
                after(V, x2)
                c(V.tensor_scalar(e[:], e[:], 1.0, None, ALU.add))
                c(V.reciprocal(sg[:], e[:]))
                per = lambda x: bc(x.unsqueeze(1).unsqueeze(3), [P, 2, 2, P])
                v4 = lambda x: x.rearrange("p (r j t) -> p r j t", r=2, j=2)
                for r in range(2):
                    w2 = lambda x: bc(x[:].unsqueeze(2), [P, 2, P])
                    half = slice(r * 256, r * 256 + 256)
                    v3 = lambda x: x.rearrange("p (j t) -> p j t", j=2)
                    kk = self.dve.done(V.tensor_tensor(kt[:, r, 1:3, :], v3(sg[:, 1, half]), w2(oml), ALU.mult))
                    c(V.tensor_tensor(v3(f1[:, half]), v3(sg[:, 0, half]), w2(oml), ALU.mult))
                    c(V.tensor_tensor(v3(f1[:, half]), v3(f1[:, half]), w2(lb), ALU.add))
                c(V.tensor_scalar(f2[:], f1[:], 1e-30, 2.0 ** -50, ALU.max, ALU.min))
                m = c(V.tensor_scalar(f1[:], f1[:], 2.0 ** -50, None, ALU.max))
                after(S, m)
                self.act.done(S.activation(f1[:], f1[:], ACT.Ln))
                x = self.act.done(S.activation(f2[:], f2[:], ACT.Ln, scale=2.0 ** 50))
                after(V, x)
                for r in range(2):
                    half = slice(r * 256, r * 256 + 256)
                    v3 = lambda x: x.rearrange("p (j t) -> p j t", j=2)
                    m = self.dve.done(V.tensor_tensor(lg[:, r, 1:3, :], v3(f1[:, half]), v3(f2[:, half]), ALU.add))
                after(V, m, self.pool.last("mixed"), self.act.last("edges"))
                for j in range(3):
                    self.dve.done(V.tensor_tensor_scan(out=b[:, 0, j, :], data0=one[:], data1=lg[:, 0, j, :], initial=0.0, op0=ALU.mult, op1=ALU.add))
                    m = self.dve.done(V.tensor_tensor_scan(out=b[:, 1, j, ::-1], data0=one[:], data1=lg[:, 1, j, ::-1], initial=0.0, op0=ALU.mult, op1=ALU.add))
                cum = m
                after(V, cum)
                self.dve.done(V.tensor_tensor(kd[:, 0], bc(b[:, 0, :, P - 1:P], [P, 3, P]), b[:, 0], ALU.subtract))
                m = self.dve.done(V.tensor_tensor(kd[:, 1], bc(b[:, 1, :, 0:1], [P, 3, P]), b[:, 1], ALU.subtract))
                after(S, m)
                dst = qd[:, bass.ds(i, 1)].rearrange("p a r j t -> p (a r) j t")
                g1 = self.act.done(S.activation(dst, b[:], ACT.Exp))
                self.act.done(S.activation(gt[:, bass.ds(i, 1), 0].rearrange("p a j -> p (a j)"), b[:, 0, :, P - 1], ACT.Exp))
                self.act.done(S.activation(gt[:, bass.ds(i, 1), 1].rearrange("p a j -> p (a j)"), b[:, 1, :, 0], ACT.Exp))
                g2 = self.act.done(S.activation(kd[:], kd[:], ACT.Exp), "edges")
                after(V, g1, g2, cq)
                self.dve.done(V.tensor_tensor(dst, dst, bc(qt[:].unsqueeze(1), [P, 2, 3, P]), ALU.mult))
                m = self.dve.done(V.tensor_tensor(kd[:], kd[:], kt[:], ALU.mult), "kd")
                after(PE, m)
                for r in range(2):
                    for j in range(3):
                        ins = PE.transpose(ps[:, 6 + r, j * P:j * P + P], kd[:, r, j, :], self.ident[:])
                tk = self.pe.done(ins)
                after(S, tk)
                m = self.act.done(S.activation(kn[:], ps[:, 6:8, 0:384], ACT.Copy))
                after(PE, m)
                vcol = ((256, 256, 0), (1312, P, 256), (1440, P, 384))
                for r in range(2):
                    for j, (col, w, at_) in enumerate(vcol):
                        ins = PE.matmul(ps[:, 6 + r, at_:at_ + w], kn[:, r, j * P:(j + 1) * P], nat[:, col:col + w], start=True, stop=True)
                um = self.pe.done(ins)
                after(G, cum)
                self.dve.done(V.tensor_tensor(mk[:, 0], kt[:, 0], kt[:, 1], ALU.add))
                self.dve.done(V.tensor_copy(mq[:, 0], qt[:]))
                mixes = []
                for l in range(1, LEVELS + 1):
                    B, s = 1 << l, l % 2
                    blk = lambda x: x.rearrange("p j (n b) -> p (j n) b", b=B)
                    n3 = 3 * P // B
                    fwd, bwd = blk(b[:, 0]), blk(b[:, 1])
                    left, right = slice(0, B // 2), slice(B // 2, B)
                    rf = bc(fwd[:, :, B // 2 - 1:B // 2], [P, n3, B // 2])
                    rb = bc(bwd[:, :, B // 2:B // 2 + 1], [P, n3, B // 2])
                    dk_, dq_ = blk(d[:, s, 0]), blk(d[:, s, 1])
                    after(G, *(mixes[-2:-1] if l > 2 else [self.dve.last("mixed"), self.dve.last("mixed0")]))
                    G.tensor_tensor(dk_[:, :, left], rf, fwd[:, :, left], ALU.subtract)
                    G.tensor_tensor(dk_[:, :, right], rb, bwd[:, :, right], ALU.subtract)
                    G.tensor_tensor(dq_[:, :, left], bwd[:, :, left], rb, ALU.subtract)
                    m = self.pool.done(G.tensor_tensor(dq_[:, :, right], fwd[:, :, right], rf, ALU.subtract), "mixed")
                    after(S, m)
                    m = self.act.done(S.activation(d[:, s], d[:, s], ACT.Exp))
                    after(V, m)
                    kf, kb = blk(kt[:, 0]), blk(kt[:, 1])
                    mkl = blk(mk[:, l])
                    self.dve.done(V.tensor_tensor(mkl[:, :, left], dk_[:, :, left], kf[:, :, left], ALU.mult))
                    self.dve.done(V.tensor_tensor(mkl[:, :, right], dk_[:, :, right], kb[:, :, right], ALU.mult))
                    mixes.append(self.dve.done(V.tensor_tensor(mq[:, l], d[:, s, 1], qt[:], ALU.mult), "mixed" if l == LEVELS else "mixed0"))
                after(V, um)
                for r in range(2):
                    uc = self.dve.done(V.tensor_tensor(u[:, bass.ds(i, 1), r].rearrange("p a n -> p (a n)"), ps[:, 6 + r, :], heads[:], ALU.mult))
                done = {}
                for (grp, l0) in ((0, 0), (1, 0), (0, 4), (1, 2), (1, 4), (1, 6)):
                    nl = 4 if grp == 0 else 2
                    prev = [v for (g2_, _), v in done.items() if g2_ == grp][-1:]
                    after(PE, mixes[max(l0 + nl - 2, 0)], *prev)
                    for l in range(l0, l0 + nl):
                        for h in range(4):
                            if grp == 0:
                                src, out = (slice(32 * h, 32 * h + 32), 0), ps[:, h, (l - l0) * P:(l - l0 + 1) * P]
                            else:
                                row = h % 2
                                src = (slice(64 * row, 64 * row + 64), 1 + h // 2)
                                q4 = (l - l0) * 2 + h // 2
                                out = ps[:, 4 + row, q4 * P:(q4 + 1) * P]
                            ins = PE.matmul(out, mk[src[0], l, src[1], :], mq[src[0], l, src[1], :], start=True, stop=True,
                                            tile_position=(src[0].start, 0))
                    mm = self.pe.done(ins)
                    after(V, mm)
                    if l0 == 0:
                        after(V, self.pe.last("av"))
                    for l in range(l0, l0 + nl):
                        if grp == 0:
                            sc = ps[:, 0:4, (l - l0) * P:(l - l0 + 1) * P]
                            dst_ = am[:, 0].rearrange("p (h t) -> p h t", h=4)
                        else:
                            sc = ps[:, 4:6, (l - l0) * 256:(l - l0 + 1) * 256].rearrange("p r (h t) -> p r h t", h=2)
                            dst_ = am[:, 1].rearrange("p (h r t) -> p r h t", h=2, r=2)
                        if l == 0:
                            msk = lmask[:, 0].unsqueeze(1) if grp == 0 else lmask[:, 0].unsqueeze(1).unsqueeze(1)
                            x = c(V.tensor_tensor(dst_, sc, bc(msk, [P, 4, P] if grp == 0 else [P, 2, 2, P]), ALU.mult))
                        else:
                            lm = lmask[:, l].bitcast(U32)
                            msk = lm.unsqueeze(1) if grp == 0 else lm.unsqueeze(1).unsqueeze(1)
                            after(V, apart=self.aside)
                            x = c(V.copy_predicated(dst_, bc(msk, [P, 4, P] if grp == 0 else [P, 2, 2, P]), sc))
                    done[grp, l0] = x
                    if (grp, l0) == (1, 6):
                        self.kit.new.named[self.kit.stage_name, "dve", "a_done"] = self.dve.n
                after(PE, done[1, 6], done[0, 4], uc)
                for h in range(8):
                    col = 256 + 64 * h if h < 4 else 1312 + 64 * (h - 4)
                    ins = PE.matmul(ps[:, 6, 64 * h:64 * h + 64], am[:, h // 4, (h % 4) * P:(h % 4 + 1) * P], nat[:, col:col + 64], start=True, stop=True)
                av = self.pe.done(ins, "av")
                self.kit.new.named[self.kit.stage_name, "pe", "nat"] = self.pe.n
                after(S, av)
                self.act.done(S.activation(o[:, bass.ds(i, 1)].rearrange("p a n -> p (a n)"), ps[:, 6, :], ACT.Copy), "o_copied")

    def scan_states(self, qd, u, gt, o):
        nc, k, ps = self.nc, self.kit, self.psum
        V = nc.vector
        k.stage("scan_states")
        channels = ((0, 0, 256), (1, 256, 384), (2, 384, 512))
        with ExitStack() as st:
            s, = self.buffers(st, [P, NT, 2, 512])
            made = {}
            for n in range(1, NT):
                for r, cur, prev in ((0, n, n - 1), (1, NT - 1 - n, NT - n)):
                    if n == 1:
                        m = self.dve.done(V.tensor_copy(s[:, cur, r], u[:, prev, r]))
                    else:
                        after(V, made[r, prev])
                        for j, a, b_ in channels:
                            m = self.dve.done(V.scalar_tensor_tensor(out=s[:, cur, r, a:b_], in0=s[:, prev, r, a:b_], scalar=gt[:, prev, r, j:j + 1],
                                                                     in1=u[:, prev, r, a:b_], op0=ALU.mult, op1=ALU.add))
                    made[r, cur] = m
            out, kept = {}, []
            for c in range(NT):
                rs = [r for r in range(2) if (r, c) in made]
                after(nc.tensor, *[made[r, c] for r in rs], *([out[c - 4]] if c >= 4 else []))
                for j, a, b_ in channels:
                    for r in rs:
                        ins = nc.tensor.matmul(ps[:, c % 4, a:b_], qd[:, c, r, j, :], s[:, c, r, a:b_], start=r == rs[0], stop=r == rs[-1])
                mm = self.pe.done(ins)
                after(V, mm)
                out[c] = self.dve.done(V.tensor_tensor(o[:, c], o[:, c], ps[:, c % 4, :], ALU.add))
                after(nc.sync, out[c])
                kept.append(self.store[c].done(nc.sync.dma_start(self.o_scan[c * P:(c + 1) * P, :], o[:, c])))
            after(nc.sync, *kept)

    def diff_prepare(self):
        nc, k, ps = self.nc, self.kit, self.psum
        V, S, G, PE = nc.vector, nc.scalar, nc.gpsimd, nc.tensor
        k.stage("diff_prepare")
        with ExitStack() as st:
            x, r, y, tmp, tr = self.buffers(st, [P, 2, D], [P, 2, 64], [P, 2, D], [P, 2, 16, 32], [P, 2, D])
            with k.rounds(NT // 2) as i:
                for s in range(2):
                    row = bass.ds(i * 2 * P + s * P, P)
                    after(nc.sync, self.dve.last(f"rot{s}"), self.pool.last(f"rot{s}"), apart=self.aside)
                    a = self.load[s].done(nc.sync.dma_start(x[:, s], self.p1[row, DQ:DQ + D]))
                    b = self.load[2 + s].done(nc.sync.dma_start(r[:, s], self.a["c_rope1"][row, :]))
                    after(V, a, b, self.pe.last(f"t{s}"))
                    after(G, a, b)
                    xv = x[:, s].rearrange("p (g c d) -> p g c d", g=16, c=2)
                    yv = y[:, s].rearrange("p (g c d) -> p g c d", g=16, c=2)
                    cos, sin = (bc(r[:, s, a_:a_ + 32].unsqueeze(1), [P, 16, 32]) for a_ in (0, 32))
                    self.dve.done(V.tensor_tensor(yv[:, :, 0], xv[:, :, 0], cos, ALU.mult))
                    m = self.dve.done(V.tensor_tensor(yv[:, :, 1], xv[:, :, 1], cos, ALU.mult))
                    after(G, self.dve.last(f"rot{s}"))
                    g1 = self.pool.done(G.tensor_tensor(tmp[:, s], xv[:, :, 1], sin, ALU.mult))
                    after(V, m, g1)
                    m = self.dve.done(V.tensor_tensor(yv[:, :, 0], yv[:, :, 0], tmp[:, s], ALU.subtract))
                    after(G, m)
                    g2 = self.pool.done(G.tensor_tensor(tmp[:, s], xv[:, :, 0], sin, ALU.mult), f"rot{s}")
                    after(V, g2)
                    m = self.dve.done(V.tensor_tensor(yv[:, :, 1], yv[:, :, 1], tmp[:, s], ALU.add), f"rot{s}")
                    after(PE, m, self.act.last(f"c{s}"), self.dve.last(f"c{s}"))
                    for j in range(8):
                        ins = PE.transpose(ps[:, 2 * s + j // 4, j % 4 * P:j % 4 * P + P], y[:, s, j * P:(j + 1) * P], self.ident[:])
                    m = self.pe.done(ins, f"t{s}")
                    after(S, m, self.store[s].last(f"s{s}"))
                    m1 = self.act.done(S.activation(tr[:, s, 0:512], ps[:, 2 * s], ACT.Copy), f"c{s}")
                    after(V, m, self.store[s].last(f"s{s}"))
                    m2 = self.dve.done(V.tensor_copy(tr[:, s, 512:1024], ps[:, 2 * s + 1]), f"c{s}")
                    after(S, m1, m2)
                    self.store[s].done(S.dma_start(self.qk_t[:, :, :, row].rearrange("c h p t -> p (c h) t"),
                                                   tr[:, s].rearrange("p (g t) -> p g t", g=8)), f"s{s}")
            after(S, *[Mark(self.store[s].sem, self.store[s].n) for s in range(2)])

    def diff_attention(self, layer):
        nc, k, ps = self.nc, self.kit, self.psum
        V, S, G, PE = nc.vector, nc.scalar, nc.gpsimd, nc.tensor
        k.stage("diff_attention")
        with ExitStack() as st:
            q, kk, v, lv, lm, lt, nm, sm, w, wt, o = self.buffers(
                st, [P, 2, T], [P, 2, T], [P, 2, NT, P], [P, 4, 64], [P, 4], [P, 1], [P, 2, 2], [P, 2, 2],
                [P, 2, 2, T], [P, 2, T], [P, 2, NT, P])
            names = ("diff_lq1", "diff_lk1", "diff_lq2", "diff_lk2")
            ld = [self.load[j].done(nc.sync.dma_start(lv[:, j], bc(self.a[n][bass.ds(layer, 1), :], [P, 64]))) for j, n in enumerate(names)]
            with nc.allow_non_contiguous_dma(reason="one value per partition"):
                ld.append(self.load[4].done(nc.sync.dma_start(lt[:], bc(self.a["c_layers"][bass.ds(layer, 1), 1:2], [P, 1]))))
            after(V, *ld)
            after(nc.sync, *ld)
            c = lambda ins: self.chain(self.dve, ins)
            for j in range(2):
                c(V.tensor_tensor(lv[:, 2 * j], lv[:, 2 * j], lv[:, 2 * j + 1], ALU.mult))
                m = c(V.reduce_sum(lm[:, j:j + 1], lv[:, 2 * j], axis=AX))
            after(S, m)
            m = self.act.done(S.activation(lm[:, 0:2], lm[:, 0:2], ACT.Exp))
            after(V, m)
            c(V.tensor_tensor(lm[:, 2:3], lm[:, 1:2], lm[:, 0:1], ALU.subtract))
            c(V.tensor_tensor(lm[:, 3:4], lm[:, 2:3], lt[:], ALU.subtract))
            with k.rounds(2) as i:
                steps = [(s, t) for s in range(2) for t in range(NT)]
                marks = {}

                def scores(n):
                    s, t = steps[n]
                    if t == 0:
                        after(nc.sync, self.pe.last(f"head{s}"), apart=self.aside)
                        a = self.load[s].done(nc.sync.dma_start(q[:, s], self.qk_t[0, bass.ds(i * 2 + s, 1)].rearrange("a p t -> (a p) t")))
                        b = self.load[2 + s].done(nc.sync.dma_start(kk[:, s], self.qk_t[1, bass.ds(i * 2 + s, 1)].rearrange("a p t -> (a p) t")))
                        d = self.load[4 + s].done(nc.sync.dma_start(v[:, s], self.p1[:, bass.ds(i * 2 * P + (DV + s * P), P)].rearrange("(n p) c -> p n c", p=P)))
                        after(PE, a, b, d)
                    after(PE, marks["exp", n - 1] if n else self.act.last("exp15"))
                    for cc in range(2):
                        rows = slice(64 * cc, 64 * cc + 64)
                        for half in range(2):
                            ins = PE.matmul(ps[:, 2 * cc + half, :], q[rows, s, t * P:(t + 1) * P], kk[rows, s, half * 512:(half + 1) * 512],
                                            start=True, stop=True, tile_position=(64 * cc, 0))
                        marks["scores", n, cc] = self.pe.done(ins)

                scores(0)
                for n, (s, t) in enumerate(steps):
                    z = n % 2
                    for cc in range(2):
                        after(V, marks["scores", n, cc], marks["exp", n - 2] if n > 1 else self.act.last(f"exp{14 + n}"))
                        m = c(V.reduce_max(nm[:, z, cc:cc + 1], ps[:, 2 * cc:2 * cc + 2, :].rearrange("p a n -> p (a n)"), axis=AX))
                        m = self.dve.done(V.tensor_scalar(nm[:, z, cc:cc + 1], nm[:, z, cc:cc + 1], -0.125, None, ALU.mult))
                        after(S, m, marks["wt", n - 2] if n > 1 else self.pe.last(f"wt{14 + n}"))
                        m = self.act.done(S.activation(w[:, z, cc], ps[:, 2 * cc:2 * cc + 2, :].rearrange("p a n -> p (a n)"), ACT.Exp,
                                                       bias=nm[:, z, cc:cc + 1], scale=0.125, accum_out=sm[:, z, cc:cc + 1]), f"exp{n}" if cc else None)
                    marks["exp", n] = m
                    if n + 1 < len(steps):
                        scores(n + 1)
                    after(V, m)
                    c(V.reciprocal(sm[:, z], sm[:, z]))
                    self.dve.done(V.tensor_scalar(w[:, z, 0], w[:, z, 0], sm[:, z, 0:1], None, ALU.mult))
                    c(V.tensor_tensor(sm[:, z, 1:2], sm[:, z, 1:2], lm[:, 3:4], ALU.mult))
                    wm = self.dve.done(V.scalar_tensor_tensor(out=w[:, z, 0], in0=w[:, z, 1], scalar=sm[:, z, 1:2], in1=w[:, z, 0], op0=ALU.mult, op1=ALU.add))
                    after(PE, wm, marks["wcopy", n - 1] if n else self.act.last("wcopy15"), marks["wcopy2", n - 1] if n else self.dve.last("wcopy15"))
                    for j in range(8):
                        ins = PE.transpose(ps[:, 4 + j // 4, j % 4 * P:j % 4 * P + P], w[:, z, 0, j * P:(j + 1) * P], self.ident[:])
                    marks["wt", n] = m = self.pe.done(ins, f"wt{n}")
                    after(S, m, marks["pv", n - 2] if n > 1 else self.pe.last(f"pv{14 + n}"))
                    marks["wcopy", n] = self.act.done(S.activation(wt[:, z, 0:512], ps[:, 4], ACT.Copy), f"wcopy{n}")
                    after(V, m, marks["pv", n - 2] if n > 1 else self.pe.last(f"pv{14 + n}"))
                    marks["wcopy2", n] = self.dve.done(V.tensor_copy(wt[:, z, 512:1024], ps[:, 5]), f"wcopy{n}")
                    after(PE, marks["wcopy", n], marks["wcopy2", n], marks["ocopy", n - 2] if n > 1 else self.act.last(f"ocopy{14 + n}"))
                    for j in range(8):
                        ins = PE.matmul(ps[:, 6 + z, 0:P], wt[:, z, j * P:(j + 1) * P], v[:, s, j, :], start=j == 0, stop=j == 7)
                    marks["pv", n] = m = self.pe.done(ins, f"pv{n}")
                    if t == NT - 1:
                        self.kit.new.named[self.kit.stage_name, "pe", f"head{s}"] = self.pe.n
                    after(S, m)
                    if t == 0:
                        after(S, self.store[s].last(f"out{s}"))
                    marks["ocopy", n] = m = self.act.done(S.activation(o[:, s, t], ps[:, 6 + z, 0:P], ACT.Copy), f"ocopy{n}")
                    if t == NT - 1:
                        after(S, m)
                        self.store[s].done(S.dma_start(self.o_diff[:, bass.ds(i * 2 * P + s * P, P)].rearrange("(n p) c -> p n c", p=P), o[:, s]), f"out{s}")
            after(S, *[Mark(self.store[s].sem, self.store[s].n) for s in range(2)])

    def merge1(self, layer):
        nc, k, ps = self.nc, self.kit, self.psum
        V, S, G, PE = nc.vector, nc.scalar, nc.gpsimd, nc.tensor
        k.stage("merge1")
        with ExitStack() as st:
            wo, hw, pw, dsc, o, g, x, sq, ss, rs, e, yt, y, ys = self.buffers(
                st, [P, KT, D], [P, D], [P, D], [P, 1], [P, 2, D], [P, 2, D], [P, 2, D], [P, D],
                [P, 2, 16], [P, 2, 16], [P, D], [P, 2, D], [P, 2, D], [P, 2])
            L = bass.ds(layer, 1)
            ld = [self.load[0].done(nc.sync.dma_start(wo[:], self.a["w_out"][L].rearrange("a (k p) n -> p (a k) n", p=P)))]
            for j, (n, w_, h0, h1) in enumerate((("gla_norm", 64, 0, 4), ("diff_norm", P, 2, 6), ("hgrn_norm", 64, 12, 16))):
                for h in range(h0, h1):
                    m = nc.sync.dma_start(hw[:, h * w_:(h + 1) * w_], bc(self.a[n][L, :], [P, w_]))
                    m = self.load[1 + j].done(m)
                    after(nc.sync, m)
                ld.append(m)
            ld.append(self.load[4].done(nc.sync.dma_start(pw[:], bc(self.a["norm_post"][L, :], [P, D]))))
            with nc.allow_non_contiguous_dma(reason="one value per partition"):
                ld.append(self.load[5].done(nc.sync.dma_start(dsc[:], bc(self.a["c_layers"][L, 2:3], [P, 1]))))
            after(V, *ld)
            after(PE, *ld)
            after(nc.sync, *ld)
            c = lambda ins: self.chain(self.dve, ins)
            c(V.tensor_scalar(hw[:, 256:768], hw[:, 256:768], dsc[:], None, ALU.mult))
            with k.rounds(NT // 2) as i:
                for s in range(2):
                    row = bass.ds(i * 2 * P + s * P, P)
                    after(nc.sync, self.pe.last(f"yt{s}"), self.dve.last(f"res{s}"), apart=self.aside)
                    for dst, src in ((o[:, s, 0:256], self.o_scan[row, 0:256]), (o[:, s, 256:768], self.o_diff[row, :]),
                                     (o[:, s, 768:1024], self.o_scan[row, 256:512]), (g[:, s, 0:256], self.p1[row, GG:GG + 256]),
                                     (g[:, s, 256:768], self.p1[row, DG:DG + 512]), (g[:, s, 768:1024], self.p1[row, HG:HG + 256]),
                                     (x[:, s], self.xs[row, :])):
                        dma = nc.sync.dma_start(dst, src)
                        m = self.load[s].done(dma)
                    after(V, m)
                    after(S, m)
                    c(V.tensor_tensor(sq[:], o[:, s], o[:, s], ALU.mult))
                    sums = lambda a_, b_, w_, h_: V.reduce_sum(ss[:, s, h_:h_ + (b_ - a_) // w_], sq[:, a_:b_].rearrange("p (h d) -> p h d", d=w_), axis=AX)
                    self.dve.done(sums(0, 256, 64, 0))
                    self.dve.done(sums(256, 768, P, 4))
                    c(sums(768, 1024, 64, 8))
                    c(V.tensor_scalar(ss[:, s, 4:8], ss[:, s, 4:8], 0.5, None, ALU.mult))
                    r = self.rstd(ss[:, s, 0:12], rs[:, s, 0:12], 1.0 / 64)
                    after(V, self.act.last("e") if s == 0 else em)
                    m = self.dve.done(V.tensor_scalar(e[:], g[:, s], -80.0, None, ALU.max))
                    after(S, m)
                    em = self.act.done(S.activation(e[:], e[:], ACT.Exp, scale=-1.0), "e" if s else None)
                    after(V, em, r)
                    c(V.tensor_scalar(e[:], e[:], 1.0, None, ALU.add))
                    c(V.reciprocal(e[:], e[:]))
                    self.dve.done(V.tensor_tensor(e[:], e[:], g[:, s], ALU.mult))
                    for a_, b_, w_, h_ in ((0, 256, 64, 0), (256, 768, P, 4), (768, 1024, 64, 8)):
                        nh = (b_ - a_) // w_
                        ov = o[:, s, a_:b_].rearrange("p (h d) -> p h d", d=w_)
                        m = self.dve.done(V.tensor_tensor(ov, ov, bc(rs[:, s, h_:h_ + nh].unsqueeze(2), [P, nh, w_]), ALU.mult))
                    after(V, m)
                    c(V.tensor_tensor(o[:, s], o[:, s], hw[:], ALU.mult))
                    m = self.dve.done(V.tensor_tensor(o[:, s], o[:, s], e[:], ALU.mult))
                    after(PE, m, self.act.last(f"yc{s}"), self.dve.last(f"yc{s}"))
                    for j in range(8):
                        ins = PE.transpose(ps[:, 4 * s + j // 4, j % 4 * P:j % 4 * P + P], o[:, s, j * P:(j + 1) * P], self.ident[:])
                    m = self.pe.done(ins, f"yt{s}")
                    after(S, m, self.pe.last(f"proj{s}"))
                    m1 = self.act.done(S.activation(yt[:, s, 0:512], ps[:, 4 * s], ACT.Copy), f"yc{s}")
                    after(V, m, self.pe.last(f"proj{s}"))
                    m2 = self.dve.done(V.tensor_copy(yt[:, s, 512:1024], ps[:, 4 * s + 1]), f"yc{s}")
                    after(PE, m1, m2, self.act.last(f"y{s}"))
                    for half in range(2):
                        for j in range(8):
                            ins = PE.matmul(ps[:, 4 * s + 2 + half], yt[:, s, j * P:(j + 1) * P], wo[:, j, half * 512:(half + 1) * 512], start=j == 0, stop=j == 7)
                    m = self.pe.done(ins, f"proj{s}")
                    after(S, m, self.store[s].last(f"out{s}"))
                    yv = ps[:, 4 * s + 2:4 * s + 4].rearrange("p a n -> p (a n)")
                    self.act.done(S.activation(y[:, s], yv, ACT.Copy), f"y{s}")
                    m = self.act.done(S.activation(yt[:, s], yv, ACT.Square, accum_out=ys[:, s:s + 1]), f"y{s}")
                    after(V, m)
                    r = self.rstd(ys[:, s:s + 1], ys[:, s:s + 1], 1.0 / D)
                    after(V, r)
                    c(V.scalar_tensor_tensor(out=y[:, s], in0=y[:, s], scalar=ys[:, s:s + 1], in1=pw[:], op0=ALU.mult, op1=ALU.mult))
                    m = self.dve.done(V.tensor_tensor(y[:, s], y[:, s], x[:, s], ALU.add), f"res{s}")
                    after(S, m)
                    self.store[s].done(S.dma_start(self.xs[row, :], y[:, s]), f"out{s}")
            after(S, *[Mark(self.store[s].sem, self.store[s].n) for s in range(2)])

    def block2(self, upto):
        self.p2 = self.dram("proj2", [T2 + 3, W2])
        self.mod = self.dram("modulation", [2, 3 * D])
        self.na_t = self.dram("na_t", [2, 4, P, T2])
        self.rpb = self.dram("rpb_rows", [120, 160])
        self.skewed = self.dram("rpb_skewed", [64, 120, 64])
        self.bias = self.dram("na_bias", [8, P, 16, 64])
        self.o_na = self.dram("o_na", [T, 512])
        self.dn = self.dram("dn_qkv", [T2 + CTX, 1536])
        self.dg = self.dram("dn_gates", [T2 + CTX, 32])
        self.o_dn = self.dram("o_dn", [2, T2, 512])
        self.modulate()
        with self.sb("h_t", [P, KT, T2]) as h_t:
            row = lambda r, j: self.mod[r:r + 1, j * D:(j + 1) * D]
            self.norm("norm_ctx", self.a["ctx_2"].rearrange("a t d -> (a t) d"), NCTX, h_t, 0, row(1, 1), row(1, 0))
            self.norm("norm2", self.xs, NT, h_t, CTX, row(0, 1), row(0, 0))
            w = self.a["w_in_2"].rearrange("a k n -> (a k) n")
            self.project("proj2_both", h_t, NT2, w, 6, BOTH // 6, self.p2, row_of=self.row2)
            self.project("proj2", h_t, NT, w, 8, (W2 - BOTH) // 8, self.p2, col0=BOTH, tok0=NCTX, row_of=self.row2)
        if upto > 5:
            self.na_bias()
            self.na_prepare("na_prep_ctx", NCTX, 0, False)
            self.na_prepare("na_prep", NT, NCTX, True)
            self.na_attention()
        if upto > 6:
            self.delta_prepare("dn_prep_ctx", NCTX, 0, False)
            self.delta_prepare("dn_prep", NT, NCTX, True)
        if upto > 7:
            self.delta_rule()
        if upto > 8:
            self.merge2()

    def modulate(self):
        nc, k, ps = self.nc, self.kit, self.psum
        V, S, G, PE = nc.vector, nc.scalar, nc.gpsimd, nc.tensor
        k.stage("modulate")
        with ExitStack() as st:
            ct, e, m, b, nw, w, z = self.buffers(st, [P, KT, 2], [P, KT, 2], [2, 3 * D], [2, 3 * D], [2, D], [P, 2, KT, 512], [P, 1536])
            with nc.allow_non_contiguous_dma(reason="two vectors"):
                ld = [self.load[2].done(nc.sync.dma_start(ct[:, :, 0], self.a["c_2"].rearrange("a (k p) -> p (a k)", p=P))),
                      self.load[3].done(nc.sync.dma_start(ct[:, :, 1], self.a["c_ctx_2"].rearrange("(k p) -> p k", p=P)))]
            ld.append(self.load[4].done(nc.sync.dma_start(b[:], bc(self.a["mod_b_2"], [2, 3 * D]))))
            ld.append(self.load[5].done(nc.sync.dma_start(nw[:], bc(self.a["norm_w_2"], [2, D]))))
            after(V, *ld)
            c = lambda ins: self.chain(self.dve, ins)
            zm = c(V.memset(z[:], 0.0))
            after(S, zm)
            for j, r in enumerate((0, CTX + 1, T2 + 2)):
                zs = self.store[j].done(S.dma_start(self.p2[r:r + 1, CONV:CONV + 1536], z[0:1, :]))
                after(S, zs)
            x = c(V.tensor_scalar(e[:], ct[:], -80.0, None, ALU.max))
            after(S, x)
            x = self.act.done(S.activation(e[:], e[:], ACT.Exp, scale=-1.0))
            after(V, x)
            c(V.tensor_scalar(e[:], e[:], 1.0, None, ALU.add))
            c(V.reciprocal(e[:], e[:]))
            x = self.dve.done(V.tensor_tensor(ct[:], ct[:], e[:], ALU.mult))
            after(PE, x)
            with k.rounds(3) as i:
                for s in range(2):
                    cols = bass.ds(i * 1024 + s * 512, 512)
                    after(nc.sync, self.pe.last(f"used{s}"), apart=self.aside)
                    wl = self.load[s].done(nc.sync.dma_start(w[:, s], self.a["mod_w_2"].rearrange("a (k p) n -> p (a k) n", p=P)[:, :, cols]))
                    after(PE, wl, self.dve.last(f"out{s}"))
                    for kt in range(KT):
                        ins = PE.matmul(ps[0:2, s, :], ct[:, kt, :], w[:, s, kt, :], start=kt == 0, stop=kt == KT - 1)
                    mm = self.pe.done(ins, f"used{s}")
                    after(V, mm)
                    o = self.dve.done(V.tensor_tensor(m[:, cols], ps[0:2, s, :], b[:, cols], ALU.add), f"out{s}")
            after(V, o)
            c(V.tensor_scalar(m[:, D:2 * D], m[:, D:2 * D], 1.0, None, ALU.add))
            x = c(V.tensor_tensor(m[:, D:2 * D], m[:, D:2 * D], nw[:], ALU.mult))
            after(nc.sync, x)
            after(nc.sync, self.store[3].done(nc.sync.dma_start(self.mod, m[:])))

    def na_bias(self):
        nc, k = self.nc, self.kit
        k.stage("na_bias")
        with ExitStack() as st:
            z, r, t, cm = self.buffers(st, [120, 160], [120, 31], [64, 120, 64], [64, 64])
            a = self.load[0].done(nc.sync.dma_start(r[:], self.a["na_rpb_2"].rearrange("a h y x -> (a h y) x")))
            b = self.load[1].done(nc.sync.dma_start(cm[:], self.a["c_cols"]))
            self.chain(self.dve, nc.vector.memset(z[:], 0.0))
            after(nc.vector, a, b)
            m = self.dve.done(nc.vector.tensor_copy(z[:, 64:95], r[:]))
            after(nc.sync, m)
            after(nc.sync, self.store[0].done(nc.sync.dma_start(self.rpb, z[:])))
            with k.rounds(64) as i:
                self.load[2].done(nc.sync.dma_start(self.skewed[bass.ds(i, 1)].rearrange("a r x -> (a r) x"), self.rpb[:, bass.ds(i * -1 + (64 + 15), 64)]))
            after(nc.sync, Mark(self.load[2].sem, self.load[2].n))
            m = self.load[3].done(nc.sync.dma_start(t[:], self.skewed))
            after(nc.vector, m)
            m = self.dve.done(nc.vector.tensor_tensor(t[:], t[:], bc(cm[:].unsqueeze(1), [64, 120, 64]), ALU.add))
            after(nc.sync, m)
            tv = t[:].rearrange("q (h y) x -> q h y x", h=8)
            for j in range(2):
                for h in range(8):
                    m = self.store[1 + j].done(nc.sync.dma_start(self.bias[h, 64 * j:64 * j + 64, j:j + 15, :], tv[:, h]))
                after(nc.sync, m)

    def na_prepare(self, name, n, first, latents):
        nc, k, ps = self.nc, self.kit, self.psum
        V, S, PE = nc.vector, nc.scalar, nc.tensor
        k.stage(name)
        nh = 16 if latents else 8
        with ExitStack() as st:
            x, w, sq, ss, rs, tr = self.buffers(st, [P, 2, D], [P, 2, 64], [P, D], [P, 2, 16], [P, 2, 16], [P, 2, D])
            ld = [self.load[4 + j].done(nc.sync.dma_start(w[:, j], bc(self.a[m], [P, 64]))) for j, m in enumerate(("na_k_norm_2", "na_q_norm_2"))]
            after(V, *ld)
            self.chain(self.dve, V.tensor_scalar(w[:, 1], w[:, 1], 0.125, None, ALU.mult))
            with k.rounds(n // 2) as i:
                for s in range(2):
                    r0 = self.row2(first + s)
                    row = bass.ds(i * 2 * P + r0, P)
                    tok = bass.ds(i * 2 * P + (first + s) * P, P)
                    after(nc.sync, self.pe.last(f"t{s}"), apart=self.aside)
                    a = self.load[s].done(nc.sync.dma_start(x[:, s, 0:512], self.p2[row, NK:NK + 512]))
                    after(V, a)
                    if latents:
                        after(V, self.load[2 + s].done(nc.sync.dma_start(x[:, s, 512:1024], self.p2[row, NQ:NQ + 512])))
                    cols = nh * 64
                    xv = x[:, s, 0:cols].rearrange("p (h d) -> p h d", d=64)
                    self.chain(self.dve, V.tensor_tensor(sq[:, 0:cols], x[:, s, 0:cols], x[:, s, 0:cols], ALU.mult))
                    self.chain(self.dve, V.reduce_sum(ss[:, s, 0:nh], sq[:, 0:cols].rearrange("p (h d) -> p h d", d=64), axis=AX))
                    r = self.rstd(ss[:, s, 0:nh], rs[:, s, 0:nh], 1.0 / 64)
                    after(V, r)
                    self.chain(self.dve, V.tensor_tensor(xv, xv, bc(rs[:, s, 0:nh].unsqueeze(2), [P, nh, 64]), ALU.mult))
                    x4 = x[:, s, 0:cols].rearrange("p (c h d) -> p c h d", h=8, d=64)
                    m = self.dve.done(V.tensor_tensor(x4, x4, bc(w[:, 0:nh // 8].unsqueeze(2), [P, nh // 8, 8, 64]), ALU.mult))
                    after(PE, m, self.act.last(f"c{s}"))
                    for j in range(nh // 2):
                        ins = PE.transpose(ps[:, 2 * s + j // 4, j % 4 * P:j % 4 * P + P], x[:, s, j * P:(j + 1) * P], self.ident[:])
                    m = self.pe.done(ins, f"t{s}")
                    after(S, m, self.store[s].last(f"k{s}"), self.store[2 + s].last(f"q{s}"))
                    banks = ps[:, 2 * s:2 * s + nh // 8].rearrange("p a n -> p (a n)")
                    m = self.act.done(S.activation(tr[:, s, 0:cols], banks, ACT.Copy), f"c{s}")
                    after(S, m)
                    four = lambda o: tr[:, s, o:o + 512].rearrange("p (h t) -> p h t", h=4)
                    self.store[s].done(S.dma_start(self.na_t[1, :, :, tok].rearrange("h p t -> p h t"), four(0)), f"k{s}")
                    if latents:
                        self.store[2 + s].done(S.dma_start(self.na_t[0, :, :, tok].rearrange("h p t -> p h t"), four(512)), f"q{s}")
            after(S, *[Mark(self.store[s].sem, self.store[s].n) for s in range(4)])

    def na_attention(self):
        nc, k, ps = self.nc, self.kit, self.psum
        V, S, G, PE = nc.vector, nc.scalar, nc.gpsimd, nc.tensor
        k.stage("na_attention")
        windows = ((0, 4, 7), (0, 4, 5), (0, 5, None), (1, 5, None), (2, 5, None), (3, 5, None), (4, 4, 3), (4, 4, 1))
        with ExitStack() as st:
            q, kk, v, bt, b5, cr, sc, nm, sm, wt, o = self.buffers(
                st, [P, T], [P, T2], [P, NT2, P], [P, 2, 14, 64], [P, 2, 10, 64], [P, 10], [P, 2, 896],
                [P, 2], [P, 2], [P, 2, 896], [P, NT, P])
            ld = self.load[5].done(nc.sync.dma_start(cr[:], self.a["c_rows"]))
            after(G, ld)
            with k.rounds(4) as i:
                after(nc.sync, self.pe.last("pv15"), self.dve.last("biased15"), self.pool.last("b5"), apart=self.aside)
                pair = bass.ds(i, 1)
                ld = [self.load[0].done(nc.sync.dma_start(q[:], self.na_t[0, pair, :, CTX:].rearrange("a p t -> (a p) t"))),
                      self.load[1].done(nc.sync.dma_start(kk[:], self.na_t[1, pair].rearrange("a p t -> (a p) t")))]
                cols = bass.ds(i * P + NV, P)
                lv = [self.load[2].done(nc.sync.dma_start(v[:, 0:NCTX], self.p2[1:1 + CTX, cols].rearrange("(n p) c -> p n c", p=P))),
                      self.load[3].done(nc.sync.dma_start(v[:, NCTX:], self.p2[CTX + 2:CTX + 2 + T, cols].rearrange("(n p) c -> p n c", p=P)))]
                lb = self.load[4].done(nc.sync.dma_start(bt[:], self.bias[bass.ds(i * 2, 2), :, 1:15, :].rearrange("a p y x -> p a y x")))
                after(PE, *ld, *lv)
                after(V, lb)
                after(G, lb, self.dve.last("biased15"))
                b5m = self.pool.done(G.tensor_tensor(b5[:], bt[:, :, 2:12, :], bc(cr[:].unsqueeze(1).unsqueeze(3), [P, 2, 10, 64]), ALU.add), "b5")
                after(V, b5m)
                steps = [(h, t) for h in range(2) for t in range(NT)]
                marks = {}

                def scores(n):
                    h, t = steps[n]
                    t0, nt, _ = windows[t]
                    z = n % 2
                    after(PE, *((marks["biased", n - 2], marks["ctx", n - 2]) if n > 1 else (self.dve.last(f"biased{14 + n}"), self.act.last(f"ctx{14 + n}"))))
                    rows = slice(64 * h, 64 * h + 64)
                    mm = lambda out, c0, c1: PE.matmul(out, q[rows, t * P:(t + 1) * P], kk[rows, c0:c1], start=True, stop=True, tile_position=(64 * h, 0))
                    key0 = CTX + t0 * P
                    mm(ps[:, 2 * z, :], key0, key0 + 512)
                    ins = mm(ps[:, 2 * z + 1, 0:CTX], 0, CTX)
                    if nt == 5:
                        ins = mm(ps[:, 2 * z + 1, CTX:CTX + P], key0 + 512, key0 + 640)
                    marks["scores", n] = self.pe.done(ins)

                scores(0)
                for n, (h, t) in enumerate(steps):
                    t0, nt, e0 = windows[t]
                    z = n % 2
                    nk = 768 + (P if nt == 5 else 0)
                    wt_prev = marks["wt", n - 2] if n > 1 else self.pe.last(f"wt{14 + n}")
                    after(V, marks["scores", n], wt_prev)
                    tab = b5[:, h] if e0 is None else bt[:, h, e0 - 1:e0 + 7]
                    m = self.dve.done(V.tensor_tensor(sc[:, z, 0:512].rearrange("p (y x) -> p y x", x=64), ps[:, 2 * z, :].rearrange("p (y x) -> p y x", x=64), tab[:, 0:8], ALU.add))
                    if nt == 5:
                        m = self.dve.done(V.tensor_tensor(sc[:, z, 768:896].rearrange("p (y x) -> p y x", x=64), ps[:, 2 * z + 1, CTX:CTX + P].rearrange("p (y x) -> p y x", x=64), tab[:, 8:10], ALU.add))
                    marks["biased", n] = m
                    if n >= 14:
                        self.kit.new.named[k.stage_name, "dve", f"biased{n}"] = self.dve.n
                    after(S, marks["scores", n], wt_prev)
                    if nt == 5:
                        after(S, m)
                    cm = marks["ctx", n] = self.act.done(S.activation(sc[:, z, 512:768], ps[:, 2 * z + 1, 0:CTX], ACT.Copy), f"ctx{n}")
                    if n + 1 < len(steps):
                        scores(n + 1)
                    after(V, m, cm)
                    m = self.chain(self.dve, V.reduce_max(nm[:, z:z + 1], sc[:, z, 0:nk], axis=AX))
                    m = self.dve.done(V.tensor_scalar(nm[:, z:z + 1], nm[:, z:z + 1], -1.0, None, ALU.mult))
                    after(S, m)
                    m = self.act.done(S.activation(sc[:, z, 0:nk], sc[:, z, 0:nk], ACT.Exp, bias=nm[:, z:z + 1], accum_out=sm[:, z:z + 1]))
                    after(PE, m, *([marks["wc", n - 1], marks["wc2", n - 1]] if n else [self.act.last("wc15"), self.dve.last("wc15")]))
                    for j in range(nk // P):
                        ins = PE.transpose(ps[:, 4 + j // 4, j % 4 * P:j % 4 * P + P], sc[:, z, j * P:(j + 1) * P], self.ident[:])
                    marks["wt", n] = tm = self.pe.done(ins, f"wt{n}")
                    pv_prev = marks["pv", n - 2] if n > 1 else self.pe.last(f"pv{14 + n}")
                    after(S, tm, pv_prev)
                    marks["wc", n] = self.act.done(S.activation(wt[:, z, 0:512], ps[:, 4], ACT.Copy), f"wc{n}")
                    after(V, tm, pv_prev)
                    marks["wc2", n] = self.dve.done(V.tensor_copy(wt[:, z, 512:nk], ps[:, 5, 0:nk - 512]), f"wc{n}")
                    after(PE, marks["wc", n], marks["wc2", n], marks["oc", n - 2] if n > 1 else self.dve.last(f"oc{14 + n}"))
                    keys = [NCTX + t0 + j for j in range(4)] + [0, 1] + ([NCTX + t0 + 4] if nt == 5 else [])
                    for j, kt in enumerate(keys):
                        ins = PE.matmul(ps[:, 6 + z, 0:64], wt[:, z, j * P:(j + 1) * P], v[:, kt, 64 * h:64 * h + 64], start=j == 0, stop=j == len(keys) - 1)
                    marks["pv", n] = pm = self.pe.done(ins, f"pv{n}")
                    after(V, m)
                    self.chain(self.dve, V.reciprocal(sm[:, z:z + 1], sm[:, z:z + 1]))
                    after(V, pm)
                    if n == 0:
                        after(V, self.store[0].last("out"))
                    om = marks["oc", n] = self.dve.done(V.tensor_scalar(o[:, t, 64 * h:64 * h + 64], ps[:, 6 + z, 0:64], sm[:, z:z + 1], None, ALU.mult), f"oc{n}")
                after(S, om)
                self.store[0].done(S.dma_start(self.o_na[:, bass.ds(i * P, P)].rearrange("(n p) c -> p n c", p=P), o[:]), "out")
            after(S, Mark(self.store[0].sem, self.store[0].n))

    def delta_prepare(self, name, n, first, latents):
        nc, k = self.nc, self.kit
        V, S, G = nc.vector, nc.scalar, nc.gpsimd
        k.stage(name)
        c = lambda ins: self.chain(self.dve, ins)
        C = 1536
        with ExitStack() as st:
            x, w, y, e, tmp, ss, rs, rp, gb, al, dt, g, sp = self.buffers(
                st, [P, 2, 3, C], [P, 3, C], [P, 2, C], [P, C], [P, C], [P, 16], [P, 16], [P, 2, 64],
                [P, 2, 32], [P, 16], [P, 16], [P, 2, 32], [P, 4, 16])
            ld = [self.load[0].done(nc.sync.dma_start(w[:], bc(self.a["conv_w_2"], [P, 3, C]))),
                  self.load[1].done(nc.sync.dma_start(al[:], bc(self.a["dn_A_log_2"].rearrange("a r h -> a (r h)"), [P, 16]))),
                  self.load[2].done(nc.sync.dma_start(dt[:], bc(self.a["dn_dt_bias_2"].rearrange("a r h -> a (r h)"), [P, 16])))]
            after(V, *ld)
            after(S, *ld)
            after(G, *ld)
            after(nc.sync, *ld)
            m = self.act.done(S.activation(al[:], al[:], ACT.Exp))
            after(V, m)
            c(V.tensor_scalar(al[:], al[:], -1.0, None, ALU.mult))
            with k.rounds(n // 2) as i:
                for s in range(2):
                    r0 = self.row2(first + s)
                    row = lambda d: bass.ds(i * 2 * P + (r0 + d), P)
                    tok = (first + s) * P
                    after(nc.sync, self.dve.last(f"conv{s}"), self.pool.last(f"conv{s}"), apart=self.aside)
                    for d in range(3):
                        m = self.load[s].done(nc.sync.dma_start(x[:, s, d], self.p2[row(d - 1), CONV:CONV + C]))
                    after(V, m)
                    after(G, m, self.dve.last("conv1") if s == 0 else sum_)
                    after(nc.sync, self.dve.last(f"g{s}"), apart=self.aside)
                    m = self.load[2 + s].done(nc.sync.dma_start(gb[:, s], self.p2[row(0), BETA:BETA + 32]))
                    after(V, m)
                    g0 = self.pool.done(G.tensor_tensor(tmp[:], x[:, s, 0], w[:, 0], ALU.mult))
                    after(V, self.store[s].last(f"qkv{s}"))
                    m = c(V.tensor_tensor(y[:, s], x[:, s, 1], w[:, 1], ALU.mult))
                    after(V, g0)
                    m = c(V.tensor_tensor(y[:, s], y[:, s], tmp[:], ALU.add))
                    after(G, m)
                    g0 = self.pool.done(G.tensor_tensor(tmp[:], x[:, s, 2], w[:, 2], ALU.mult), f"conv{s}")
                    after(V, g0)
                    sum_ = m = self.chain(self.dve, V.tensor_tensor(y[:, s], y[:, s], tmp[:], ALU.add))
                    self.kit.new.named[k.stage_name, "dve", f"conv{s}"] = self.dve.n
                    m = c(V.tensor_scalar(e[:], y[:, s], -80.0, None, ALU.max))
                    after(S, m)
                    m = self.act.done(S.activation(e[:], e[:], ACT.Exp, scale=-1.0))
                    after(V, m)
                    c(V.tensor_scalar(e[:], e[:], 1.0, None, ALU.add))
                    c(V.reciprocal(e[:], e[:]))
                    c(V.tensor_tensor(y[:, s], y[:, s], e[:], ALU.mult))
                    qk = y[:, s, 0:1024].rearrange("p (h d) -> p h d", d=64)
                    c(V.tensor_tensor(e[:, 0:1024], y[:, s, 0:1024], y[:, s, 0:1024], ALU.mult))
                    c(V.reduce_sum(ss[:], e[:, 0:1024].rearrange("p (h d) -> p h d", d=64), axis=AX))
                    r = self.rstd(ss[:], rs[:], 1.0)
                    after(V, r)
                    c(V.tensor_scalar(rs[:, 0:8], rs[:, 0:8], 0.125, None, ALU.mult))
                    m = c(V.tensor_tensor(qk, qk, bc(rs[:].unsqueeze(2), [P, 16, 64]), ALU.mult))
                    if latents:
                        after(nc.sync, self.dve.last(f"rot{s}"), apart=self.aside)
                        m = self.load[4 + s].done(nc.sync.dma_start(rp[:, s], self.a["c_rope2"][bass.ds(i * 2 * P + s * P, P), :]))
                        after(V, m)
                        for a_ in range(2):
                            half = y[:, s, 0:1024].rearrange("p (h a c d) -> p h a c d", a=2, c=2, d=16)[:, :, a_]
                            x1, x2 = half[:, :, 0], half[:, :, 1]
                            cos, sin = (bc(rp[:, s, o_ + 16 * a_:o_ + 16 * a_ + 16].unsqueeze(1), [P, 16, 16]) for o_ in (0, 32))
                            t4 = e[:, 0:1024].rearrange("p (j h d) -> p j h d", j=4, d=16)
                            self.dve.done(V.tensor_tensor(t4[:, 0], x1, cos, ALU.mult))
                            self.dve.done(V.tensor_tensor(t4[:, 1], x2, sin, ALU.mult))
                            self.dve.done(V.tensor_tensor(t4[:, 2], x2, cos, ALU.mult))
                            c(V.tensor_tensor(t4[:, 3], x1, sin, ALU.mult))
                            self.dve.done(V.tensor_tensor(x1, t4[:, 0], t4[:, 1], ALU.subtract))
                            m = c(V.tensor_tensor(x2, t4[:, 2], t4[:, 3], ALU.add))
                        self.kit.new.named[k.stage_name, "dve", f"rot{s}"] = self.dve.n
                    qm = m
                    gv, go = gb[:, s], g[:, s]
                    after(V, self.store[2 + s].last(f"gates{s}"))
                    m = c(V.tensor_scalar(sp[:, 0], gv[:, 0:16], -80.0, None, ALU.max))
                    c(V.tensor_tensor(sp[:, 2], gv[:, 16:32], dt[:], ALU.add))
                    m = c(V.tensor_scalar(sp[:, 1], sp[:, 2], -1.0, None, ALU.mult))
                    m = c(V.tensor_tensor(sp[:, 1], sp[:, 1], sp[:, 2], ALU.min))
                    after(S, m)
                    self.act.done(S.activation(sp[:, 0], sp[:, 0], ACT.Exp, scale=-1.0))
                    m = self.act.done(S.activation(sp[:, 1], sp[:, 1], ACT.Exp))
                    after(V, m)
                    c(V.tensor_scalar(sp[:, 0], sp[:, 0], 1.0, None, ALU.add))
                    self.dve.done(V.reciprocal(go[:, 0:16], sp[:, 0]))
                    c(V.tensor_scalar(sp[:, 3], sp[:, 1], 2.0, None, ALU.add))
                    c(V.reciprocal(sp[:, 3], sp[:, 3]))
                    c(V.tensor_tensor(sp[:, 1], sp[:, 1], sp[:, 3], ALU.mult))
                    c(V.tensor_tensor(sp[:, 3], sp[:, 1], sp[:, 1], ALU.mult))
                    c(V.tensor_scalar(sp[:, 0], sp[:, 3], 1.0 / 17, None, ALU.mult))
                    for d in (15, 13, 11, 9, 7, 5, 3):
                        c(V.scalar_tensor_tensor(out=sp[:, 0], in0=sp[:, 0], scalar=1.0 / d, in1=sp[:, 3], op0=ALU.add, op1=ALU.mult))
                    c(V.scalar_tensor_tensor(out=sp[:, 0], in0=sp[:, 0], scalar=1.0, in1=sp[:, 1], op0=ALU.add, op1=ALU.mult))
                    c(V.tensor_scalar(sp[:, 2], sp[:, 2], 0.0, None, ALU.max))
                    c(V.scalar_tensor_tensor(out=sp[:, 0], in0=sp[:, 0], scalar=2.0, in1=sp[:, 2], op0=ALU.mult, op1=ALU.add))
                    gm = self.dve.done(V.tensor_tensor(go[:, 16:32], sp[:, 0], al[:], ALU.mult), f"g{s}")
                    after(S, qm, gm)
                    for base in ([tok] if latents else [tok, tok + T2]):
                        rows = bass.ds(i * 2 * P + base, P)
                        self.store[s].done(S.dma_start(self.dn[rows, :], y[:, s]), f"qkv{s}")
                        self.store[2 + s].done(S.dma_start(self.dg[rows, :], go), f"gates{s}")
            after(S, *[Mark(self.store[s].sem, self.store[s].n) for s in range(4)])

    def delta_rule(self):
        nc, k, ps = self.nc, self.kit, self.psum
        V, S, G, PE = nc.vector, nc.scalar, nc.gpsimd, nc.tensor
        k.stage("delta")
        c = lambda ins: self.chain(self.dve, ins)
        N = T2 // 64
        with ExitStack() as st:
            (ones, x, gb, sums, tri, gm, gd, dec, ex, gt, kb, vb, kbg, qg, kd, tq, tk, lt, qk, ct, xm, xt, ym, um, wt, vn, sm, o) = self.buffers(
                st, [P, P], [P, 2, 1536], [P, 2, 16], [P, 3, P], [P, 8, 64], [P, 512], [P, 16], [P, 512], [P, 16],
                [P, 8], [P, 512], [P, 512], [P, 512], [P, 512], [P, 512], [P, 4, 3, P], [P, 4, P],
                [P, 512], [P, 512], [P, 6, 512], [P, 512], [P, 512], [P, 512], [P, 512], [P, 2, 256], [P, 512],
                [P, 2, 256], [P, 2, 512])
            h3 = lambda t: t.rearrange("p (h d) -> p h d", h=8)
            a = self.load[6].done(nc.sync.dma_start(sums[:], self.a["c_sums"]))
            b = self.load[7].done(nc.sync.dma_start(tri[:], self.a["c_tri"]))
            for e in (V, PE, G, nc.sync):
                after(e, a, b)
            c(V.memset(gd[:], 0.0))
            c(V.memset(ones[:], 1.0))
            m0 = c(V.memset(sm[:], 0.0))
            after(PE, m0)
            halves = (slice(0, 64), slice(64, P))
            eye = bc(tri[:, 7].unsqueeze(1), [P, 8, 64])

            def product(bank, left, right):
                for r, rows in enumerate(halves):
                    for h in range(8):
                        cols = slice(64 * h, 64 * h + 64)
                        ins = PE.matmul(ps[rows, bank + r, cols], left[rows, cols], right[rows, cols], start=True, stop=True)
                return ins

            with k.rounds(N // 2) as i:
                for s in range(2):
                    cf = bass.ds(i * 128 + s * 64, 64)
                    cb = bass.ds(i * -128 + (CTX + 64 * (N - 1) - s * 64), 64)
                    after(nc.sync, self.dve.last(f"x{s}"), self.pe.last(f"x{s}"), apart=self.aside)
                    for j, cr in enumerate((cf, cb)):
                        rows = halves[j]
                        m = self.load[s].done(nc.sync.dma_start(x[rows, s], self.dn[cr, :]))
                        self.load[2 + s].done(nc.sync.dma_start(gb[rows, s, 0:8], self.dg[cr, 8 * j:8 * j + 8]))
                        m2 = self.load[2 + s].done(nc.sync.dma_start(gb[rows, s, 8:16], self.dg[cr, 16 + 8 * j:24 + 8 * j]))
                    q_, k_, v_ = x[:, s, 0:512], x[:, s, 512:1024], x[:, s, 1024:1536]
                    beta, g = gb[:, s, 0:8], gb[:, s, 8:16]
                    per = lambda t: bc(t.unsqueeze(2), [P, 8, 64])
                    after(V, m, m2, self.pe.last("decay") if s == 0 else decay)
                    self.dve.done(V.tensor_copy(gd[0:64, 0:8], g[0:64]))
                    self.dve.done(V.tensor_copy(gd[64:128, 8:16], g[64:128]))
                    m = self.dve.done(V.tensor_tensor(h3(gm[:]), bc(tri[:, 0].unsqueeze(1), [P, 8, 64]), per(g), ALU.mult))
                    after(PE, m, *([self.act.last("o1"), self.dve.last("o2"), self.dve.last("state")] if s == 0 else [o1, o2, state]), apart=self.aside)
                    PE.matmul(ps[:, 0, :], sums[:, 0], gm[:], start=True, stop=True)
                    PE.matmul(ps[:, 1, 0:8], sums[:, 1], g, start=True, stop=True)
                    PE.matmul(ps[:, 1, 8:16], sums[:, 0], g, start=True, stop=True)
                    ins = PE.matmul(ps[:, 1, 16:32], ones[:], gd[:], start=True, stop=True)
                    decay = m = self.pe.done(ins, "decay" if s else None)
                    after(S, m, *([self.dve.last("state"), self.dve.last("kd")] if s == 0 else [state, kdm]))
                    self.act.done(S.activation(dec[:], ps[:, 0, :], ACT.Exp))
                    for j, rows in enumerate(halves):
                        self.act.done(S.activation(gt[rows].rearrange("p (r h) -> p r h", r=2), ps[rows, 1, 16:32].rearrange("p (r h b) -> p r h b", r=2, b=2)[:, :, :, j], ACT.Exp))
                    m = self.act.done(S.activation(ex[:], ps[:, 1, 0:16], ACT.Exp))
                    kbm = self.dve.done(V.tensor_tensor(h3(kb[:]), h3(k_), per(beta), ALU.mult))
                    self.dve.done(V.tensor_tensor(h3(vb[:]), h3(v_), per(beta), ALU.mult))
                    after(V, m, kbm)
                    self.dve.done(V.tensor_tensor(h3(qg[:]), h3(q_), per(ex[:, 0:8]), ALU.mult))
                    self.dve.done(V.tensor_tensor(h3(kbg[:]), h3(kb[:]), per(ex[:, 0:8]), ALU.mult))
                    kdm = m = self.dve.done(V.tensor_tensor(h3(kd[:]), h3(k_), per(ex[:, 8:16]), ALU.mult), "kd" if s else None)
                    self.kit.new.named[k.stage_name, "dve", f"x{s}"] = self.dve.n
                    m2 = self.dve.done(V.tensor_tensor(h3(dec[:]), h3(dec[:]), bc(tri[:, 0].unsqueeze(1), [P, 8, 64]), ALU.mult))
                    after(PE, m, apart=self.aside)
                    for bank, src in ((2, k_), (3, kb[:]), (4, q_), (5, qg[:])):
                        for j in range(4):
                            ins = PE.transpose(ps[:, bank, j * P:(j + 1) * P], src[:, j * P:(j + 1) * P], self.ident[:])
                    m = self.pe.done(ins, f"x{s}")
                    after(S, m)
                    self.act.done(S.activation(tk[:], ps[:, 2, :].rearrange("p (j t) -> p j t", j=4), ACT.Copy))
                    ca = self.act.done(S.activation(tq[:, :, 0], ps[:, 3, :].rearrange("p (j t) -> p j t", j=4), ACT.Copy))
                    after(V, m)
                    cv = self.dve.done(V.tensor_copy(tq[:, :, 1:3].rearrange("p j b t -> p b j t"), ps[:, 4:6, :].rearrange("p b (j t) -> p b j t", j=4)))
                    after(PE, ca, cv, apart=self.aside)
                    for par, hr in enumerate(halves):
                        for r, dr in enumerate(halves):
                            for j in range(4):
                                ins = PE.matmul(ps[dr, 6 + par, j * P:(j + 1) * P], tk[hr, j, dr], tq[hr, j, 0:2, dr], start=True, stop=True,
                                                tile_position=(64 * par, 64 * r))
                    m = self.pe.done(ins)
                    after(V, m, m2)
                    heads = lambda t: t.rearrange("p (h b d) -> p b h d", b=2, h=4)
                    both = ps[:, 6:8, :].rearrange("p b (h c d) -> p b c h d", c=2, d=64)
                    for b_ in range(2):
                        hv = lambda t: t.rearrange("p (h b d) -> p b h d", b=2, h=4)[:, b_]
                        self.dve.done(V.tensor_tensor(hv(lt[:]), both[:, b_, 0], hv(dec[:]), ALU.mult))
                    lm = self.dve.n
                    for b_ in range(2):
                        hv = lambda t: t.rearrange("p (h b d) -> p b h d", b=2, h=4)[:, b_]
                        qkm = self.dve.done(V.tensor_tensor(hv(qk[:]), both[:, b_, 1], hv(dec[:]), ALU.mult))
                    lm = Mark(self.dve.sem, self.dve.base + lm)
                    after(G, lm)
                    cts = {}
                    for l in range(2, 7):
                        cts[l] = self.pool.done(G.tensor_tensor(h3(ct[:, l - 1]), h3(lt[:]), bc(tri[:, l].unsqueeze(1), [P, 8, 64]), ALU.mult))
                    after(V, lm)
                    m = c(V.tensor_tensor(h3(ct[:, 0]), h3(lt[:]), bc(tri[:, 1].unsqueeze(1), [P, 8, 64]), ALU.mult))
                    xtm = self.dve.done(V.tensor_tensor(h3(xt[:]), eye, h3(ct[:, 0]), ALU.subtract))
                    after(PE, m, apart=self.aside)
                    for r, rows in enumerate(halves):
                        for h in range(8):
                            cols = slice(64 * h, 64 * h + 64)
                            ins = PE.matmul(ps[rows, r, cols], ct[rows, 0, cols], tri[rows, 7], start=True, stop=True)
                    m = self.pe.done(ins)
                    after(V, m)
                    for r, rows in enumerate(halves):
                        xmm = self.dve.done(V.tensor_tensor(h3(xm[rows]), bc(tri[rows, 7].unsqueeze(1), [64, 8, 64]), h3(ps[rows, r, :]), ALU.subtract))
                    for l in range(2, 7):
                        after(PE, xmm, cts[l], apart=self.aside)
                        m = self.pe.done(product(0, ct[:, l - 1], xm))
                        after(S, m)
                        y1 = self.act.done(S.activation(ym[0:64], ps[0:64, 0, :], ACT.Copy))
                        after(V, m)
                        y2 = self.dve.done(V.tensor_copy(ym[64:128], ps[64:128, 1, :]))
                        after(PE, y1, y2, xtm, apart=self.aside)
                        if l < 6:
                            m = self.pe.done(product(2, xt, ym))
                            after(V, m)
                            for r, rows in enumerate(halves):
                                xmm = self.dve.done(V.tensor_tensor(xm[rows], xm[rows], ps[rows, 2 + r, :], ALU.subtract))
                        m = self.pe.done(product(4, ym, xt))
                        after(V, m)
                        for r, rows in enumerate(halves):
                            xtm = self.dve.done(V.tensor_tensor(xt[rows], xt[rows], ps[rows, 4 + r, :], ALU.subtract))
                    after(PE, xtm, apart=self.aside)
                    m = self.pe.done(product(0, xt, vb))
                    after(S, m)
                    self.act.done(S.activation(um[0:64], ps[0:64, 0, :], ACT.Copy))
                    ua = self.act.done(S.activation(um[64:128], ps[64:128, 1, :], ACT.Copy))
                    for r, dr in enumerate(halves):
                        for par, hr in enumerate(halves):
                            for j in range(4):
                                h = 2 * j + par
                                ins = PE.matmul(ps[hr, 2 + r, 64 * j:64 * j + 64], kbg[dr, 64 * h:64 * h + 64], xt[dr, 64 * h:64 * h + 64], start=True, stop=True,
                                                tile_position=(64 * r, 64 * par))
                    m = self.pe.done(ins)
                    after(V, m)
                    m = self.dve.done(V.tensor_copy(wt[:], ps[:, 2:4, 0:256]))
                    after(PE, m, self.dve.last("state") if s == 0 else state, qkm, apart=self.aside)

                    def with_state(bank, left):
                        for par, hr in enumerate(halves):
                            for r, dr in enumerate(halves):
                                for j in range(4):
                                    ins = PE.matmul(ps[dr, bank + par, 64 * j:64 * j + 64], left(hr, r, dr, j), sm[hr, r, 64 * j:64 * j + 64], start=True, stop=True,
                                                    tile_position=(64 * par, 64 * r))
                        return self.pe.done(ins)
                    m = with_state(6, lambda hr, r, dr, j: wt[hr, r, 64 * j:64 * j + 64])
                    oo = with_state(4, lambda hr, r, dr, j: tq[hr, j, 2, dr])
                    after(V, m, ua)
                    vm = self.dve.done(V.tensor_tensor(heads(vn[:]), heads(um[:]), ps[:, 6:8, 0:256].rearrange("p b (h d) -> p b h d", h=4), ALU.subtract))
                    after(S, oo, self.store[s].last(f"o{s}"))
                    o1 = self.act.done(S.activation(heads(o[:, s]), ps[:, 4:6, 0:256].rearrange("p b (h d) -> p b h d", h=4), ACT.Copy), "o1" if s else None)
                    after(PE, vm, apart=self.aside)
                    om = self.pe.done(product(0, qk, vn))
                    for r, dr in enumerate(halves):
                        for par, hr in enumerate(halves):
                            for j in range(4):
                                h = 2 * j + par
                                ins = PE.matmul(ps[hr, 2 + r, 64 * j:64 * j + 64], kd[dr, 64 * h:64 * h + 64], vn[dr, 64 * h:64 * h + 64], start=True, stop=True,
                                                tile_position=(64 * r, 64 * par))
                    m = self.pe.done(ins)
                    after(V, oo)
                    c(V.tensor_tensor(sm[:].rearrange("p r (h d) -> p (r h) d", d=64), sm[:].rearrange("p r (h d) -> p (r h) d", d=64), bc(gt[:].unsqueeze(2), [P, 8, 64]), ALU.mult))
                    after(V, m)
                    state = self.dve.done(V.tensor_tensor(sm[:], sm[:], ps[:, 2:4, 0:256], ALU.add), "state" if s else None)
                    after(V, om, o1, state)
                    for r, rows in enumerate(halves):
                        o2 = self.dve.done(V.tensor_tensor(o[rows, s], o[rows, s], ps[rows, r, :], ALU.add), "o2" if s else None)
                    after(S, o2)
                    self.store[s].done(S.dma_start(self.o_dn[0, cf, :], o[0:64, s]), f"o{s}")
                    self.store[s].done(S.dma_start(self.o_dn[1, bass.ds(i * -128 + (64 * (N - 1) - s * 64), 64), :], o[64:128, s]), f"o{s}")
            after(S, *[Mark(self.store[s].sem, self.store[s].n) for s in range(2)])

    def merge2(self):
        nc, k, ps = self.nc, self.kit, self.psum
        V, S, G, PE = nc.vector, nc.scalar, nc.gpsimd, nc.tensor
        k.stage("merge2")
        c = lambda ins: self.chain(self.dve, ins)
        with ExitStack() as st:
            wb, wo, nw, gate, o, ob, z, x, e, ss, rs, yt, y = self.buffers(
                st, [P, 8, D], [P, 8, D], [P, 64], [P, D], [P, D], [P, 512], [P, 3 * D], [P, 2, D], [P, 3 * D],
                [P, 8], [P, 8], [P, D], [P, 2, D])
            kp = lambda n: self.a[n].rearrange("a (k p) n -> p (a k) n", p=P)
            ld = [self.load[0].done(nc.sync.dma_start(wb[:, 0:4], kp("w_o_na_2"))), self.load[1].done(nc.sync.dma_start(wb[:, 4:8], kp("w_o_dn_2"))),
                  self.load[2].done(nc.sync.dma_start(wo[:], kp("w_out_2"))), self.load[3].done(nc.sync.dma_start(nw[:], bc(self.a["dn_norm_w_2"], [P, 64]))),
                  self.load[4].done(nc.sync.dma_start(gate[:], bc(self.mod[0:1, 2 * D:3 * D], [P, D])))]
            for e_ in (V, PE, nc.sync):
                after(e_, *ld)
            with k.rounds(NT // 2) as i:
                for s in range(2):
                    row = lambda d: bass.ds(i * 2 * P + (s * P + d), P)
                    after(nc.sync, *([self.dve.last("gated"), self.pe.last("branches_t"), self.dve.last(f"y{s}")] if s == 0 else [gated, bt, self.dve.last(f"y{s}")]), apart=self.aside)
                    for dst, src in ((o[:, 0:512], self.o_na[row(0), :]), (o[:, 512:1024], self.o_dn[0, row(CTX), :]), (ob[:], self.o_dn[1, row(0), :]),
                                     (z[:], self.p2[row(CTX + 2), NZ:NZ + 3 * D])):
                        m = self.load[0].done(nc.sync.dma_start(dst, src))
                    after(nc.sync, self.dve.last(f"out{s}"), apart=self.aside)
                    xl = self.load[1 + s].done(nc.sync.dma_start(x[:, s], self.xs[row(0), :]))
                    after(V, m, xl)
                    m = c(V.tensor_scalar(e[:], z[:], -80.0, None, ALU.max))
                    after(S, m)
                    m = self.act.done(S.activation(e[:], e[:], ACT.Exp, scale=-1.0))
                    c(V.tensor_tensor(o[:, 512:1024], o[:, 512:1024], ob[:], ALU.add))
                    c(V.tensor_tensor(ob[:], o[:, 512:1024], o[:, 512:1024], ALU.mult))
                    c(V.reduce_sum(ss[:], ob[:].rearrange("p (h d) -> p h d", d=64), axis=AX))
                    r = self.rstd(ss[:], rs[:], 1.0 / 64)
                    after(V, m, r)
                    c(V.tensor_scalar(e[:], e[:], 1.0, None, ALU.add))
                    c(V.reciprocal(e[:], e[:]))
                    gated = self.dve.done(V.tensor_tensor(z[:, 0:D], z[:, 0:D], e[:, 0:D], ALU.mult), "gated")
                    ov = o[:, 512:1024].rearrange("p (h d) -> p h d", d=64)
                    c(V.tensor_tensor(ov, ov, bc(rs[:].unsqueeze(2), [P, 8, 64]), ALU.mult))
                    c(V.tensor_tensor(ov, ov, bc(nw[:].unsqueeze(1), [P, 8, 64]), ALU.mult))
                    gated = m = self.dve.done(V.tensor_tensor(o[:], o[:], z[:, 0:D], ALU.mult), "gated")
                    after(PE, m, *([self.act.last("ytc"), self.dve.last("fin")] if s == 0 else [ytc, fin]))

                    def transposed(src, bank):
                        for j in range(8):
                            ins = PE.transpose(ps[:, bank + j // 4, j % 4 * P:j % 4 * P + P], src[:, j * P:(j + 1) * P], self.ident[:])
                        m = self.pe.done(ins, "branches_t")
                        after(S, m)
                        mm = self.act.done(S.activation(yt[:], ps[:, bank:bank + 2].rearrange("p a n -> p (a n)"), ACT.Copy), "ytc")
                        after(PE, mm)
                        return m, mm
                    bt, ytc = transposed(o, 0)
                    for b_ in range(2):
                        for half in range(2):
                            for j in range(4):
                                ins = PE.matmul(ps[:, 2 + 2 * b_ + half], yt[:, (4 * b_ + j) * P:(4 * b_ + j + 1) * P], wb[:, 4 * b_ + j, half * 512:(half + 1) * 512],
                                                start=j == 0, stop=j == 3)
                    m = self.pe.done(ins)
                    after(V, m, self.store[s].last(f"o{s}"))
                    two = lambda b_: ps[:, b_:b_ + 2].rearrange("p a n -> p (a n)")
                    self.dve.done(V.tensor_tensor(y[:, s], two(2), e[:, D:2 * D], ALU.mult))
                    c(V.tensor_tensor(e[:, 2 * D:3 * D], two(4), e[:, 2 * D:3 * D], ALU.mult))
                    m = self.dve.done(V.tensor_tensor(y[:, s], y[:, s], e[:, 2 * D:3 * D], ALU.add))
                    after(PE, m)
                    _, ytc = transposed(y[:, s], 6)
                    for half in range(2):
                        for j in range(8):
                            ins = PE.matmul(ps[:, 2 + half], yt[:, j * P:(j + 1) * P], wo[:, j, half * 512:(half + 1) * 512], start=j == 0, stop=j == 7)
                    m = self.pe.done(ins)
                    after(V, m)
                    fin = c(V.tensor_tensor(y[:, s], two(2), gate[:], ALU.mult))
                    self.kit.new.named[k.stage_name, "dve", "fin"] = self.dve.n
                    m = self.dve.done(V.tensor_tensor(y[:, s], y[:, s], x[:, s], ALU.add), f"out{s}")
                    self.kit.new.named[k.stage_name, "dve", f"y{s}"] = self.dve.n
                    after(S, m)
                    self.store[s].done(S.dma_start(self.out[0, row(0), :], y[:, s]), f"o{s}")
            after(S, *[Mark(self.store[s].sem, self.store[s].n) for s in range(2)])


def build(nc, args, out, old, upto=99):
    return Program(nc, args, out, old).build(upto)


def counts(make, upto=99):
    nc, args, out = make()
    return build(nc, args, out, Book(), upto)


def kernel(**inputs):
    import concourse.bacc as bacc
    from concourse.bass_utils import run_bass_kernel_spmd as run

    arrays = {n: np.asarray(a) for n, a in inputs.items()}
    w = arrays["w_in_2"]
    cut = lambda a, b: w[:, :, a:b]
    arrays["w_in_2"] = np.concatenate([cut(512, 1536), cut(2048, 3584), cut(4096, 4128), cut(0, 512), cut(1536, 2048),
                                       cut(3584, 4096), cut(4128, 6176)], axis=2)
    arrays.update(constants())
    arrays = {n: np.ascontiguousarray(a) for n, a in arrays.items()}

    def make():
        nc = bacc.Bacc("TRN2", target_bir_lowering=False, num_devices=1)
        args = {n: nc.dram_tensor(f"in_{n}", a.shape, F32, kind="ExternalInput").ap() for n, a in arrays.items()}
        return nc, args, nc.dram_tensor("out_x", (1, T, D), F32, kind="ExternalOutput").ap()

    book = counts(make)
    nc, args, out = make()
    build(nc, args, out, book)
    r = run(nc, [{f"in_{n}": a for n, a in arrays.items()}], core_ids=[0])
    return r.results[0]["out_x"]
```
